# Optimizing a Trainium2 kernel written in Bass

```python
import math
import jax, jax.numpy as jnp
from jax import lax
import numpy as np

D_MODEL = 2048
BATCH = 1
SEQ = 256
DEPTH = 1
DEC_BATCH = 8
DEC_SEQ = 1
PAST_LEN = 2048
PAGE_SIZE = 128

N_QK_HEADS = 16
N_V_HEADS = 32
HEAD_K = 128
HEAD_V = 128
KEY_DIM = N_QK_HEADS * HEAD_K
VAL_DIM = N_V_HEADS * HEAD_V
QKV_DIM = 2 * KEY_DIM + VAL_DIM
QKV_CONV = 4
CHUNK = 64
SC_DIM = D_MODEL
SC_CONV = 3
D_FF = ((8 * D_MODEL // 3 + 255) // 256) * 256
PLE_DIM = 256
EPS = 1e-6

IN_SIZES = (KEY_DIM, KEY_DIM, VAL_DIM, VAL_DIM, N_V_HEADS, N_V_HEADS,
            SC_DIM, SC_DIM, SC_DIM, D_MODEL, D_MODEL)
IN_DIM = sum(IN_SIZES)
IN_SPLITS = tuple(int(s) for s in np.cumsum(IN_SIZES)[:-1])

kernel_name = "hybrid_gdn_shortconv_decode_step"

def rmsnorm(x, g):
    xf = x.astype(jnp.float32)
    r = xf * lax.rsqrt(jnp.mean(xf * xf, axis=-1, keepdims=True) + EPS)
    return (r * g.astype(jnp.float32)).astype(x.dtype)

def l2norm(x):
    return x * lax.rsqrt(jnp.sum(x * x, axis=-1, keepdims=True) + EPS)

def causal_dwconv(x, buf, w):
    K = w.shape[0]
    T = x.shape[1]
    xp = jnp.concatenate([buf.astype(x.dtype), x], axis=1)
    y = sum(w[j].astype(x.dtype) * xp[:, j:j + T] for j in range(K))
    return y, xp[:, -(K - 1):]

def gated_delta_rule(q, k, v, g, beta, s0):
    Bn, T, H, Dk = q.shape
    Dv = v.shape[-1]
    n_chunks = -(-T // CHUNK)
    pad = n_chunks * CHUNK - T

    def prep(a):
        a = jnp.pad(a, [(0, 0), (0, pad)] + [(0, 0)] * (a.ndim - 2))
        a = a.reshape((Bn, n_chunks, CHUNK) + a.shape[2:])
        return jnp.moveaxis(a, 3, 1)

    q = prep(q) * (HEAD_K ** -0.5)
    k = prep(k)
    v = prep(v)
    g = prep(g)
    beta = prep(beta)
    G = jnp.cumsum(g, axis=-1)
    idx = jnp.arange(CHUNK)
    lower = idx[:, None] >= idx[None, :]
    strict = idx[:, None] > idx[None, :]
    decay = jnp.exp(jnp.where(lower, G[..., :, None] - G[..., None, :], -jnp.inf))
    kk = jnp.einsum('bhncd,bhnsd->bhncs', k, k)
    A = jnp.where(strict, beta[..., :, None] * kk * decay, 0.0)
    eye = jnp.eye(CHUNK, dtype=A.dtype)
    rhs = jnp.concatenate([v * beta[..., None], k * (beta * jnp.exp(G))[..., None]], axis=-1)
    sol = lax.linalg.triangular_solve(eye + A, rhs, left_side=True, lower=True)
    u = sol[..., :Dv]
    w = sol[..., Dv:]
    qk = jnp.einsum('bhncd,bhnsd->bhncs', q, k) * decay

    def step(S, xs):
        q_c, k_c, u_c, w_c, G_c, qk_c = xs
        u_new = u_c - jnp.einsum('bhcd,bhde->bhce', w_c, S)
        o = (jnp.einsum('bhcd,bhde->bhce', q_c * jnp.exp(G_c)[..., None], S)
             + jnp.einsum('bhcs,bhse->bhce', qk_c, u_new))
        G_last = G_c[..., -1]
        S = (S * jnp.exp(G_last)[..., None, None]
             + jnp.einsum('bhcd,bhce->bhde', k_c * jnp.exp(G_last[..., None] - G_c)[..., None], u_new))
        return S, o

    xs = tuple(jnp.moveaxis(a, 2, 0) for a in (q, k, u, w, G, qk))
    S, o = lax.scan(step, s0, xs)
    o = jnp.moveaxis(jnp.moveaxis(o, 0, 2), 1, 3).reshape(Bn, n_chunks * CHUNK, H, Dv)[:, :T]
    return o, S

def layer(h, p_i, s_gdn, s_qkv, s_sc,
          attn_norm, w_in, qkv_conv_w, a_log, dt_bias, gdn_norm, w_gdn_out,
          sconv_w, w_sconv_out, w_o, ffn_norm, w_ffn_gate, w_ffn_up, w_ffn_down,
          ple_norm, w_ple_gate, w_ple_proj):
    Bn, T, _ = h.shape
    dt = h.dtype
    xn = rmsnorm(h, attn_norm)
    proj = xn @ w_in
    q, k, v, z, a, b, sB, sC, sh, gA, gB = jnp.split(proj, IN_SPLITS, axis=-1)

    qkv, new_qkv = causal_dwconv(jnp.concatenate([q, k, v], axis=-1), s_qkv, qkv_conv_w)
    qkv = jax.nn.silu(qkv).astype(jnp.float32)
    q, k, v = jnp.split(qkv, (KEY_DIM, 2 * KEY_DIM), axis=-1)
    rep = N_V_HEADS // N_QK_HEADS
    q = jnp.repeat(l2norm(q.reshape(Bn, T, N_QK_HEADS, HEAD_K)), rep, axis=2)
    k = jnp.repeat(l2norm(k.reshape(Bn, T, N_QK_HEADS, HEAD_K)), rep, axis=2)
    v = v.reshape(Bn, T, N_V_HEADS, HEAD_V)
    beta = jax.nn.sigmoid(b.astype(jnp.float32))
    g = -jnp.exp(a_log.astype(jnp.float32)) * jax.nn.softplus(a.astype(jnp.float32) + dt_bias.astype(jnp.float32))
    o, S = gated_delta_rule(q, k, v, g, beta, s_gdn.astype(jnp.float32))
    o = rmsnorm(o, gdn_norm) * jax.nn.silu(z.reshape(Bn, T, N_V_HEADS, HEAD_V).astype(jnp.float32))
    y_a = o.reshape(Bn, T, VAL_DIM).astype(dt) @ w_gdn_out

    conv, new_sc = causal_dwconv(sC * sh, s_sc, sconv_w)
    y_b = (sB * conv) @ w_sconv_out

    mixed = jax.nn.sigmoid(gA) * y_a + jax.nn.sigmoid(gB) * y_b
    h = h + mixed @ w_o

    hn = rmsnorm(h, ffn_norm)
    h = h + (jax.nn.silu(hn @ w_ffn_gate) * (hn @ w_ffn_up)) @ w_ffn_down

    hn = rmsnorm(h, ple_norm)
    h = h + jax.nn.sigmoid(hn @ w_ple_gate) * (p_i.astype(dt) @ w_ple_proj)
    return h, S.astype(s_gdn.dtype), new_qkv.astype(s_qkv.dtype), new_sc.astype(s_sc.dtype)

def setup_inputs(seed: int = 0) -> dict:
    key = jax.random.key(seed)
    ks = jax.random.split(key, 32)
    f32 = jnp.float32

    def nrm(k, shape, scale):
        return jax.random.normal(k, shape, f32) * scale

    def gain(k, shape):
        return 1.0 + 0.02 * jax.random.normal(k, shape, f32)

    return {
        "x_prompt": nrm(ks[0], (BATCH, SEQ, D_MODEL), 1.0),
        "x_sample": nrm(ks[1], (DEC_BATCH, DEC_SEQ, D_MODEL), 1.0),
        "state_gdn": nrm(ks[2], (DEPTH, DEC_BATCH, N_V_HEADS, HEAD_K, HEAD_V), 0.05),
        "state_qkv_conv": nrm(ks[3], (DEPTH, DEC_BATCH, QKV_CONV - 1, QKV_DIM), 1.0),
        "state_short_conv": nrm(ks[4], (DEPTH, DEC_BATCH, SC_CONV - 1, SC_DIM), 1.0),
        "p_prompt": nrm(ks[5], (DEPTH, BATCH, SEQ, PLE_DIM), 1.0),
        "p_sample": nrm(ks[6], (DEPTH, DEC_BATCH, DEC_SEQ, PLE_DIM), 1.0),
        "attn_norm": gain(ks[7], (DEPTH, D_MODEL)),
        "w_in": nrm(ks[8], (DEPTH, D_MODEL, IN_DIM), D_MODEL ** -0.5),
        "qkv_conv_w": nrm(ks[9], (DEPTH, QKV_CONV, QKV_DIM), QKV_CONV ** -0.5),
        "a_log": jnp.log(jax.random.uniform(ks[10], (DEPTH, N_V_HEADS), f32, 1.0, 16.0)),
        "dt_bias": nrm(ks[11], (DEPTH, N_V_HEADS), 0.1),
        "gdn_norm": gain(ks[12], (DEPTH, HEAD_V)),
        "w_gdn_out": nrm(ks[13], (DEPTH, VAL_DIM, D_MODEL), VAL_DIM ** -0.5),
        "sconv_w": nrm(ks[14], (DEPTH, SC_CONV, SC_DIM), SC_CONV ** -0.5),
        "w_sconv_out": nrm(ks[15], (DEPTH, SC_DIM, D_MODEL), SC_DIM ** -0.5),
        "w_o": nrm(ks[16], (DEPTH, D_MODEL, D_MODEL), D_MODEL ** -0.5),
        "ffn_norm": gain(ks[17], (DEPTH, D_MODEL)),
        "w_ffn_gate": nrm(ks[18], (DEPTH, D_MODEL, D_FF), D_MODEL ** -0.5),
        "w_ffn_up": nrm(ks[19], (DEPTH, D_MODEL, D_FF), D_MODEL ** -0.5),
        "w_ffn_down": nrm(ks[20], (DEPTH, D_FF, D_MODEL), D_FF ** -0.5),
        "ple_norm": gain(ks[21], (DEPTH, D_MODEL)),
        "w_ple_gate": nrm(ks[22], (DEPTH, D_MODEL, D_MODEL), D_MODEL ** -0.5),
        "w_ple_proj": nrm(ks[23], (DEPTH, PLE_DIM, D_MODEL), PLE_DIM ** -0.5),
        "final_norm": gain(ks[24], (D_MODEL,)),
    }

def reference(x_prompt, x_sample, state_gdn, state_qkv_conv, state_short_conv, p_prompt, p_sample,
              attn_norm, w_in, qkv_conv_w, a_log, dt_bias, gdn_norm, w_gdn_out, sconv_w, w_sconv_out,
              w_o, ffn_norm, w_ffn_gate, w_ffn_up, w_ffn_down, ple_norm, w_ple_gate, w_ple_proj,
              final_norm):
    nb = x_prompt.shape[0]
    dt = x_prompt.dtype
    zero_gdn = jnp.zeros((nb, N_V_HEADS, HEAD_K, HEAD_V), dt)
    zero_qkv = jnp.zeros((nb, QKV_CONV - 1, QKV_DIM), dt)
    zero_sc = jnp.zeros((nb, SC_CONV - 1, SC_DIM), dt)
    hp, hs = x_prompt, x_sample
    gdn_p, qkv_p, sc_p, gdn_s, qkv_s, sc_s = [], [], [], [], [], []
    for i in range(DEPTH):
        lw = (attn_norm[i], w_in[i], qkv_conv_w[i], a_log[i], dt_bias[i], gdn_norm[i], w_gdn_out[i],
              sconv_w[i], w_sconv_out[i], w_o[i], ffn_norm[i], w_ffn_gate[i], w_ffn_up[i], w_ffn_down[i],
              ple_norm[i], w_ple_gate[i], w_ple_proj[i])
        hp, s1, s2, s3 = layer(hp, p_prompt[i], zero_gdn, zero_qkv, zero_sc, *lw)
        gdn_p.append(s1); qkv_p.append(s2); sc_p.append(s3)
        hs, s1, s2, s3 = layer(hs, p_sample[i], state_gdn[i], state_qkv_conv[i], state_short_conv[i], *lw)
        gdn_s.append(s1); qkv_s.append(s2); sc_s.append(s3)
    y_prompt = rmsnorm(hp, final_norm)
    y_sample = rmsnorm(hs, final_norm)
    return (y_prompt, y_sample, jnp.stack(gdn_p), jnp.stack(qkv_p), jnp.stack(sc_p),
            jnp.stack(gdn_s), jnp.stack(qkv_s), jnp.stack(sc_s))


_drawn_inputs = setup_inputs


def setup_inputs(seed=0):
    import zlib

    import numpy as np

    out = dict(_drawn_inputs(seed))
    spreads = {}
    factors = {'gdn_norm': 8.0, 'ffn_norm': 4.616, 'ple_norm': 8.0, 'final_norm': 2.832}
    for name, (base, spread) in spreads.items():
        noise = np.random.default_rng([zlib.crc32(name.encode()), seed]).standard_normal(out[name].shape)
        drawn = base * np.exp(spread * noise) if base else spread * noise
        out[name] = __import__('jax').numpy.asarray(drawn.astype(out[name].dtype))
    for name, factor in factors.items():
        out[name] = (out[name] * factor).astype(out[name].dtype)
    return out
```

```python
from contextlib import ExitStack

import concourse.bass as bass
from concourse import mybir

F32 = mybir.dt.float32
F32R = mybir.dt.float32r
I8 = mybir.dt.int8
ALU = mybir.AluOpType
ACT = mybir.ActivationFunctionType
ds = bass.ds

P = 128
COLS = 256
KT = 4
RAW = 8
SPLIT = 4
AHEAD = 3
CH = 128
EPS = 1e-6
MASKED = -1.0e30


class Count:

    def __init__(self, sem):
        self.sem, self.base, self.k, self.it, self.per = sem, 0, 0, None, 0

    def enter(self, it, per):
        self.base, self.k, self.it, self.per = self.base + self.k, 0, it, per

    def leave(self, iters):
        assert self.k == self.per, f"{self.k} increments in the body, not {self.per}"
        self.base, self.k, self.it = self.base + self.per * iters, 0, None

    def inc(self, ins):
        ins.then_inc(self.sem, 1)
        self.k += 1
        return ins

    def settle(self, eng):
        v = self.base + self.k
        eng.wait_ge(self.sem, v if self.it is None else self.it * self.per + v)


class Pair:

    def __init__(self, rows, col, kts, rhs, tiles=2, kind="", arg=0, kt0=0, xready=None):
        self.rows, self.col, self.kts, self.rhs, self.tiles = rows, col, kts, rhs, tiles
        self.kind, self.arg, self.kt0, self.xready = kind, arg, kt0, xready


class Phase:
    def __init__(self, name, iters, pairs):
        self.name, self.iters, self.pairs = name, iters, pairs
        self.pieces = sum(len(q.kts) for q in pairs)
        assert iters == 1 or (self.pieces % RAW == 0 and len(pairs) % 2 == 0), name


def trunk(nc, I, O):
    D = I["w_in"].shape[1]
    T = I["x_prompt"].shape[1]
    NB = I["x_sample"].shape[0]
    N = T + NB
    DT = D // P
    HV = I["state_gdn"].shape[2]
    QKV = I["state_qkv_conv"].shape[3]
    VAL = HV * P
    KEY = (QKV - VAL) // 2
    HK = KEY // P
    F = I["w_ffn_gate"].shape[2]
    FT = F // P
    HALF = FT // 2
    PD = I["w_ple_proj"].shape[1]
    NG = HK // 2
    Z0, A0 = QKV, QKV + VAL
    SB0 = A0 + 2 * HV
    SC0, SH0 = SB0 + D, SB0 + 2 * D
    GA0, GB0 = SB0 + 3 * D, SB0 + 4 * D
    NPB = DT // 2
    QSCALE = float(P) ** -0.5
    BLK = T // P
    NCH = T // CH
    assert NCH == 2 and NG == NPB == 8 and NB == 8

    base = (nc.sbuf_base + 63) // 64 * 64
    top = [base]

    def at(name, shape, dt, offset):
        return nc.alloc_sbuf_tensor_at(name, list(shape), dt, offset=offset)

    def size(shape, dt):
        n = 1 if dt is I8 else 4
        for s in shape[1:]:
            n *= s
        return (n + 31) // 32 * 32

    def new(name, shape, dt=F32):
        t = at(name, shape, dt, top[0])
        top[0] += size(shape, dt)
        return t

    raw = new("raw", [P, RAW, KT, COLS])
    whi = new("whi", [P, SPLIT, KT, COLS], F32R)
    wlo = new("wlo", [P, SPLIT, KT, COLS], F32R)
    xhi = new("xhi", [P, DT, N], F32R)
    xlo = new("xlo", [P, DT, N], F32R)
    join = new("join", [P, 7, CH], I8)
    joinT = new("joinT", [P, 7, CH], I8)
    ident = new("ident", [P, P])
    ones = new("ones", [P, P])
    later = new("later", [P, CH])
    vec = new("vec", [P, 369])
    rstd = new("rstd", [P, N])
    eps = new("eps", [P, 1])
    tok = new("tok", [P, 5, NCH, HV])
    bc = new("bc", [P, 1 + 2 * NB, HV])
    smp = new("smp", [P, 64, NB])
    regO = top[0]
    o_all = new("o_all", [P, HV, N])
    yb = new("yb", [P, DT, N])
    regT = top[0]
    sqk = new("sqk", [P, 4, N])
    sv = new("sv", [P, 4, N])
    kTok = new("kTok", [P, NCH, 2, P])
    vTok = new("vTok", [P, NCH, 4, P])
    GW = new("GW", [P, 10, 4 * CH])
    EG = new("EG", [P, 4, CH])
    S = new("S", [P, 4, P])
    cin = new("cin", [P, 2, 292])
    cacc = new("cacc", [P, 2, 288])
    scb = new("scb", [P, 2, N])
    tail = new("tail", [P, 10, 11])
    st_qkv = new("st_qkv", [24, 2, 2, P])
    st_sc = new("st_sc", [16, 2, P])
    Gc = new("Gc", [32, T])
    end = nc.sbuf_usable_end
    end = end() if callable(end) else end
    assert top[0] <= end, (top[0], end)
    stg2 = scb
    stg = vTok
    hpro = at("hpro", [P, DT, N], F32, regO)
    sqr = at("sqr", [P, DT, N], F32, regO + size([P, HV, N], F32))
    xrow = at("xrow", [P, BLK + 1, D], F32, regT)
    vrow = at("vrow", [P, 3, P], F32, regT + size([P, BLK + 1, D], F32))
    prep = at("prep", [64, 11, N], F32, regT + size([P, BLK + 1, D], F32) + 2048)
    dgs = at("dgs", [32, 1 + 2 * NB, HV], F32, regT)
    sgA = at("sgA", [P, DT, N], F32, regT)
    sgB = at("sgB", [P, DT, N], F32, regT + 4 * DT * N)
    regS = regT + 8 * DT * N
    chunkS = at("chunkS", [P, 2, 16, P], F32, regS)
    kqs = at("kqs", [P, HK, NB, 2], F32, regS + 16384)
    so = at("so", [P, 5, NB, HV], F32, regS)
    dTs = at("dTs", [P, 2, P], F32, regS + 8192)
    sq2 = at("sq2", [P, 2, 2 * HK, NB], F32, regT)
    assert regS + 16384 + 1024 <= end
    h = at("h", [P, DT, N], F32, regT)
    pp = at("pp", [P, DT, N], F32, regT + 4 * DT * N)
    sS = at("sS", [P, 2, 16, P], F32, regT + 4 * DT * N)
    sD = at("sD", [P, 2, 16, P], F32, regT + 4 * DT * N + 16384)
    ahi = at("ahi", [P, HALF, N], F32R, regO)
    alo = at("alo", [P, HALF, N], F32R, regO + 4 * HALF * N)
    et = at("et", [P, 4, N], F32, regO + 8 * HALF * N)
    assert 8 * HALF * N + 16 * N <= 4 * (HV + DT) * N
    sqh = at("sqh", [P, DT, N], F32, regO)
    prow = at("prow", [P, BLK + 1, PD], F32, regS)
    phi = at("phi", [P, PD // P, N], F32R, regS + 4096)
    plo = at("plo", [P, PD // P, N], F32R, regS + 8192)
    yrow = at("yrow", [P, BLK + 1, D], F32, regO + 4 * DT * N)

    hT_d = nc.dram_tensor("h_scratch", [P, DT * N], F32).ap()
    dT_d = nc.dram_tensor("d_scratch", [NB * HV, P], F32).ap()

    ctx = ExitStack()
    with ctx:
        bank = [ctx.enter_context(nc.psum_tensor(f"bank{i}", [P, 512], F32)) for i in range(8)]

        def sem(name):
            return ctx.enter_context(nc.semaphore(name))

        raw_loaded = [sem(f"raw_loaded{i}") for i in range(RAW)]
        hi_ready, lo_ready, piece_used = sem("hi_ready"), sem("lo_ready"), sem("piece_used")
        pair_free = [sem("pair_free0"), sem("pair_free1")]
        xhi_ready, xlo_ready = sem("xhi_ready"), sem("xlo_ready")
        sq_ready, sum_ready, mean_ready, rstd_ready = sem("sq_ready"), sem("sum_ready"), sem("mean_ready"), sem("rstd_ready")
        act_self, dve_self, pool_self = sem("act_self"), sem("dve_self"), sem("pool_self")
        pool_passed, dve_passed = sem("pool_passed"), sem("dve_passed")
        ident_ready = sem("ident_ready")
        consts_ready, x_in, v_in, vec_turned, vec_ready = (sem(n) for n in ("consts_ready", "x_in", "v_in", "vec_turned", "vec_ready"))
        x_turned, h_copied, h_stored, col_in = (sem(n) for n in ("x_turned", "h_copied", "h_stored", "col_in"))
        soft_in, soft_ready, g_ready, rows_ready = (
            sem(n) for n in ("soft_in", "soft_ready", "g_ready", "rows_ready"))
        ea_ready, diag_ready, tok_turned = (sem(n) for n in ("ea_ready", "diag_ready", "tok_turned"))
        z_scaled = sem("z_scaled")
        conv_done, silu_done = sem("conv_done"), sem("silu_done")
        sconv_done, yb_ready = sem("sconv_done"), sem("yb_ready")
        st_in = [sem("st_in0"), sem("st_in1")]
        st_turned, sc_in, sc_turned = sem("st_turned"), sem("sc_in"), sem("sc_turned")
        tails_turned, tails_staged, tails_stored = sem("tails_turned"), sem("tails_staged"), sem("tails_stored")
        sct_turned, sct_staged, sct_stored = sem("sct_turned"), sem("sct_staged"), sem("sct_stored")
        rows_left = sem("rows_left")
        g = {n: sem("g_" + n) for n in (
            "squares", "gsel", "sums", "log", "gb", "root", "dt", "qkn", "kkqk", "turned", "copied",
            "lt", "lt_turned", "vturned", "x", "y", "ycopied", "xy", "u0", "u0s", "s1", "s1c", "ks", "r",
            "expo", "xinit", "u1", "u1s", "o1", "s2", "stored", "osq", "osum", "olog", "oroot", "o")}
        gate_scaled = sem("gate_scaled")
        s_in = [sem("s_in0"), sem("s_in1")]
        s_used, kq_ready, kq_sq, kq_sum, kq_rec, kq_root = (sem(n) for n in ("s_used", "kq_ready", "kq_sq", "kq_sum", "kq_rec", "kq_root"))
        kq_prod, kq_dot, d_ready, d_turned, d_rows, d_stored = (sem(n) for n in ("kq_prod", "kq_dot", "d_ready", "d_turned", "d_rows", "d_stored"))
        so_sq, so_sum, so_rec, so_root, so_done = (sem(n) for n in ("so_sq", "so_sum", "so_rec", "so_root", "so_done"))
        n_in = [sem("n_in0"), sem("n_in1")]
        n_scaled, n_done = sem("n_scaled"), sem("n_done")
        n_stored = [sem("n_stored0"), sem("n_stored1")]
        h_in = sem("h_in")
        fg_scaled, a_hi, a_ready = sem("fg_scaled"), sem("a_hi"), sem("a_ready")
        p_in, p_turned, pg_scaled, pg_done = sem("p_in"), sem("p_turned"), sem("pg_scaled"), sem("pg_done")
        y_ready, y_turned, y_copied, out_stored, states_shifted = (sem(n) for n in ("y_ready", "y_turned", "y_copied", "out_stored", "states_shifted"))

        win = I["w_in"].rearrange("o (k p) n -> p (o k) n", p=P)
        wga = I["w_gdn_out"].rearrange("o (k p) n -> p (o k) n", p=P)
        wsc = I["w_sconv_out"].rearrange("o (k p) n -> p (o k) n", p=P)
        wo = I["w_o"].rearrange("o (k p) n -> p (o k) n", p=P)
        wfg = I["w_ffn_gate"].rearrange("o (k p) n -> p (o k) n", p=P)
        wfu = I["w_ffn_up"].rearrange("o (k p) n -> p (o k) n", p=P)
        wfd = I["w_ffn_down"].rearrange("o (k p) n -> p (o k) n", p=P)
        wpg = I["w_ple_gate"].rearrange("o (k p) n -> p (o k) n", p=P)
        wpp = I["w_ple_proj"].rearrange("o (k p) n -> p (o k) n", p=P)
        X = (xhi, xlo)
        K4 = [KT] * (DT // KT)

        XR = {n: i * DT for i, n in enumerate(("attn", "yb", "o0", "o1", "mix", "ffn"))}
        XR["ple_p"] = 6 * DT
        XR["ple"] = 6 * DT + PD // P

        def mk(rows, col, rhs, kind, arg=0, kts=K4, tiles=2, kt0=0, xr=None):
            return Pair(rows, col, kts, rhs, tiles, kind, arg, kt0, xr)

        def qkvpair(kind, gx):
            if kind[0] == "v":
                p = int(kind[1])
                return mk(win, lambda it, f=gx: 2 * KEY + f(it) * 512 + p * COLS, X, "qkv", ("v", p, gx), xr="attn")
            b = {"q": 0, "k": KEY}[kind]
            return mk(win, lambda it, f=gx: b + f(it) * COLS, X, "qkv", (kind, 0, gx), xr="attn")

        def zpair(p, gx):
            return mk(win, lambda it: Z0 + gx(it) * 512 + p * COLS, X, "z", (p, gx), xr="attn")

        def spair(kind, b, gx):
            return mk(win, lambda it: b + gx(it) * COLS, X, kind, gx, xr="attn")

        nxt, cur = (lambda it: it + 1), (lambda it: it)
        const = lambda n: (lambda it: n)
        QKVS = ("v0", "v1", "q", "k")
        phases = [
            Phase("first", 1, [mk(win, lambda it: A0, X, "ab", tiles=1, xr="attn")] + [qkvpair(k, const(0)) for k in QKVS] + [zpair(p, const(0)) for p in range(2)]),
            Phase("groups", NG - 1, [spair("sc", SC0, cur), spair("sh", SH0, cur), qkvpair("v0", nxt), qkvpair("v1", nxt),
                                     zpair(0, nxt), qkvpair("q", nxt), qkvpair("k", nxt), zpair(1, nxt)]),
            Phase("last_group", 1, [spair("sc", SC0, const(NG - 1)), spair("sh", SH0, const(NG - 1))]
                  + [spair("sb", SB0, const(i)) for i in range(6)]),
            Phase("sb", 1, [spair("sb", SB0, const(i)) for i in range(6, NPB)]),
            Phase("gates", NPB, [spair("gate", GA0, cur), spair("gate", GB0, cur)]),
            Phase("yb0", 1, [mk(wsc, lambda it, n=n: n * COLS, X, "yb", const(n), xr="yb") for n in range(4)]),
            Phase("yb1", 2, [mk(wsc, lambda it, n=n: (2 * it + 4 + n) * COLS, X, "yb", (lambda it, n=n: 2 * it + 4 + n), xr="yb") for n in range(2)]),
            Phase("ya0", 4, [mk(wga, lambda it, n=n: (2 * it + n) * COLS, X, "ya", (lambda it, n=n: 2 * it + n), xr="o0") for n in range(2)]),
            Phase("ya1", 4, [mk(wga, lambda it, n=n: (2 * it + n) * COLS, X, "ya", (lambda it, n=n: 2 * it + n), kt0=DT, xr="o1") for n in range(2)]),
            Phase("wo", 4, [mk(wo, lambda it, n=n: (2 * it + n) * COLS, X, "addh", (lambda it, n=n: 2 * it + n), xr="mix") for n in range(2)]),
        ]
        A = (ahi, alo)
        FP = HALF // 2
        down = [3] * 6 + [2] * 2
        assert sum(down) == HALF
        for half in range(2):
            for part, lo_, n_ in (("r", 0, FP - NB), ("s", FP - NB, NB)):
                gx = lambda it, lo_=lo_, half=half: it * 2 + (half * FP + lo_)
                ax = lambda it, lo_=lo_: it * 2 + lo_
                name = f"ffn{half}{part}"
                phases.append(Phase(name, n_ // 2 if part == "s" else 1, sum([[
                    mk(wfg, lambda it, gx=gx, r=r: (gx(it) + r) * COLS, X, "fg", (ax, half, r), xr="ffn"),
                    mk(wfu, lambda it, gx=gx, r=r: (gx(it) + r) * COLS, X, "fu", (ax, half, r), xr="ffn")]
                    for r in range(2 if part == "s" else n_)], [])))
            phases.append(Phase(f"down{half}", 4, [mk(wfd, lambda it, n=n: (2 * it + n) * COLS, A, "addh", (lambda it, n=n: 2 * it + n),
                                                      kts=down, kt0=half * HALF, xr=f"act{half}") for n in range(2)]))
        phases.append(Phase("pproj", 1, [mk(wpp, lambda it, n=n: n * COLS, (phi, plo), "pp", const(n), kts=[PD // P], xr="ple_p") for n in range(NPB)]))
        phases.append(Phase("pgate_first", 1, [mk(wpg, lambda it, n=n: n * COLS, X, "pg", const(n), xr="ple") for n in range(2)]))
        phases.append(Phase("pgate", NPB // 2 - 2, [mk(wpg, lambda it, n=n: (2 * it + n) * COLS, X, "pg", (lambda it, n=n: 2 * it + n), xr="ple") for n in (2, 3)]))
        phases.append(Phase("pgate_last", 1, [mk(wpg, lambda it, n=n: n * COLS, X, "pg", const(n), xr="ple") for n in (NPB - 2, NPB - 1)]))
        pc = qc = 0
        for ph in phases:
            ph.p0, ph.q0 = pc, qc
            pc += ph.pieces * ph.iters
            qc += len(ph.pairs) * ph.iters
        PIECES = pc
        by = {ph.name: ph for ph in phases}

        def mul(it, n, c):
            return it * n + c

        def walk(eng, work, counts=(), per=None):
            for ph in phases:
                work("before", ph, 0)
                if ph.iters == 1:
                    work("body", ph, 0)
                else:
                    with eng.Fori(0, ph.iters) as it:
                        for c in counts:
                            c.enter(it, per[ph.name])
                        work("body", ph, it)
                    for c in counts:
                        c.leave(ph.iters)

        def group_of(ph, it):
            return it if ph.name == "groups" else NG - 1 if ph.name == "last_group" else None

        def piece(ph, it, j):
            return it * ph.pieces + (ph.p0 + j + 1)

        def freed(eng, ph, it, i):
            n = ph.q0 + i
            eng.wait_ge(pair_free[n % 2], it * (len(ph.pairs) // 2) + (n // 2 + 1))

        def freed_all(eng, ph):
            n = ph.q0 + ph.iters * len(ph.pairs) - 1
            for m in (n - 1, n):
                eng.wait_ge(pair_free[m % 2], m // 2 + 1)

        LEVELS = {p: (p - 3,) for p in range(8, 20)}
        PE_STEP = {0: (0,), 1: ("decay",), 2: (1,), 5: (3,), 7: (4,), **LEVELS, 20: (17, 23), 21: (18,), 22: (19,), 23: (20,),
                   24: (21,), 26: (22,)}
        ACT_STEP = {0: (0,), 3: (1,), 4: (2,), 5: (3,), 7: (4,), **LEVELS, 21: (23, 18), 24: (21,), 27: (22,)}
        DVE_STEP = {0: ("decay",), 2: ("exponents",), 4: (2,), 5: (3,), 7: (4,), **LEVELS, 20: (17,), 22: (19,), 23: (20,),
                    24: (21,), 29: (23,)}
        NORM = {"first": 0, "ffn0r": 1, "pgate_first": 2}
        LV = 7

        def half(v, lv, side):
            s = 1 << lv
            return v.rearrange("p (m t) -> p m t", t=2 * s)[:, :, side * s:(side + 1) * s]
        PREV = lambda ph: phases[phases.index(ph) - 1]

        def vcol(i):
            return vec[:, ds(i, 1)]

        block = ctx.enter_context(nc.Block())

        @block.sync
        def _(sp):
            for b in range(BLK):
                sp.dma_start(xrow[:, b, :], I["x_prompt"][0, b * P:(b + 1) * P, :]).then_inc(x_in, 16)
            sp.dma_start(xrow[0:NB, BLK, :], I["x_sample"][:, 0, :]).then_inc(x_in, 16)

            def body(ph, it):
                j = 0
                for q in ph.pairs:
                    kt = q.kt0
                    for n in q.kts:
                        p = ph.p0 + j
                        if p >= RAW:
                            sp.wait_ge(lo_ready, mul(it, ph.pieces, p - RAW + 1))
                        sp.dma_start(raw[:, p % RAW, 0:n, :], q.rows[:, kt:kt + n, ds(q.col(it), COLS)]).then_inc(raw_loaded[p % RAW], 16)
                        kt += n
                        j += 1

            for ph in phases:
                if ph.iters == 1:
                    body(ph, 0)
                else:
                    with sp.Fori(0, ph.iters) as it:
                        body(ph, it)
            yo = O["y_prompt"]
            for b in range(BLK):
                sp.wait_ge(y_copied, DT // 4 * (b + 1))
                sp.dma_start(yo[0, b * P:(b + 1) * P, :], yrow[:, b, :]).then_inc(out_stored, 16)
            sp.wait_ge(y_copied, DT // 4 * (BLK + 1))
            sp.dma_start(O["y_sample"][:, 0, :], yrow[0:NB, BLK, :]).then_inc(out_stored, 16)
            sp.wait_ge(out_stored, 16 * (BLK + 1))
            sp.wait_ge(h_stored, 16)
            sp.wait_ge(d_stored, 32)
            sp.wait_ge(g["stored"], 16 * NG)
            sp.wait_ge(tails_stored, 16 * 6 * NG)
            sp.wait_ge(sct_stored, 32 * NG)
            sp.wait_ge(states_shifted, 32)
            for i in range(2):
                sp.wait_ge(n_stored[i], 16 * NB)


        @block.gpsimd
        def _(pool):
            mine = Count(pool_self)
            pool.sem_inc(rows_left, 1)
            mine.inc(pool.memset(ident[:, :], 0.0))
            mine.inc(pool.memset(ones[:, :], 1.0))
            mine.inc(pool.memset(eps[:, :], EPS))
            mine.settle(pool)
            pool.affine_select(out=ident[:, :], in_=ident[:, :], compare_op=ALU.not_equal, fill=1.0, base=0,
                               pattern=[[-1, P]], channel_multiplier=1).then_inc(ident_ready, 1)
            mine.inc(pool.memset(later[:, :], 0.0))
            mine.inc(pool.memset(join[:, :, :], 0))
            mine.inc(pool.memset(joinT[:, :, :], 0))
            mine.inc(pool.memset(cin[:, :, 0:3], 0.0))
            mine.settle(pool)
            mine.inc(pool.affine_select(out=later[:, :], in_=later[:, :], compare_op=ALU.is_ge, fill=MASKED, base=0,
                                        pattern=[[1, CH]], channel_multiplier=-1))
            views = []
            for lv in range(7):
                s = 1 << lv
                nb = CH // (2 * s)
                for m, off, lo_, hi_ in ((join, 0, -s, 2 * s - 1), (joinT, s, 0, s - 1)):
                    v = m[:, lv, :].rearrange("p (b t) -> p b t", b=nb)[:, :, off:off + s]
                    views.append((v, nb, s, lo_, hi_))
                    mine.inc(pool.memset(v, 1))
            mine.settle(pool)
            for v, nb, s, lo_, hi_ in views:
                mine.inc(pool.affine_select(out=v, in_=v, compare_op=ALU.is_ge, fill=0.0, base=lo_,
                                            pattern=[[-2 * s, nb], [0, s]], channel_multiplier=1))
            mine.settle(pool)
            for v, nb, s, lo_, hi_ in views:
                mine.inc(pool.affine_select(out=v, in_=v, compare_op=ALU.is_ge, fill=0.0, base=hi_,
                                            pattern=[[2 * s, nb], [0, s]], channel_multiplier=-1))
            mine.settle(pool)
            pool.nop().then_inc(consts_ready, 1)
            pool.wait_ge(h_copied, DT)
            pool.dma_start(hT_d, hpro[:, :, :].rearrange("p k t -> p (k t)")).then_inc(h_stored, 16)
            pool.dma_start(O["qkv_s"][0, :, 0:2, :], I["state_qkv_conv"][0, :, 1:3, :]).then_inc(states_shifted, 16)
            pool.dma_start(O["sc_s"][0, :, 0:1, :], I["state_short_conv"][0, :, 1:2, :]).then_inc(states_shifted, 16)

            stq = I["state_qkv_conv"][0].rearrange("b j n -> (b j) n")
            sts = I["state_short_conv"][0].rearrange("b j n -> (b j) n")

            def load_states(grp, after):
                for i, col in enumerate((2 * KEY + grp * 512, 2 * KEY + grp * 512 + COLS, grp * COLS, KEY + grp * COLS)):
                    if after is not None or i >= 2:
                        pool.wait_ge(st_turned, (after if after is not None else 0) + i - 1)
                        pool.sem_inc(pool_passed, 1)
                    pool.dma_start(st_qkv[:, i % 2, :, :], stq[:, ds(col, COLS)].rearrange("r (t p) -> r t p", p=P)).then_inc(st_in[i % 2], 16)

            def group(grp, last):
                pool.wait_ge(sc_turned, grp + 1)
                pool.sem_inc(pool_passed, 1)
                pool.dma_start(st_sc[:, :, :], sts[:, ds(grp * COLS, COLS)].rearrange("r (t p) -> r t p", p=P)).then_inc(sc_in, 16)
                pool.wait_ge(tails_staged, grp + 1)
                pool.sem_inc(pool_passed, 1)
                rows = stg[:, :, :, :].rearrange("p a b c -> p (a b c)")
                for s0, col, n in ((0, 2 * KEY + grp * 512, 512), (512, grp * COLS, COLS), (768, KEY + grp * COLS, COLS)):
                    pool.dma_start(O["qkv_p"][0, 0, :, ds(col, n)], rows[0:3, s0:s0 + n]).then_inc(tails_stored, 16)
                    pool.dma_start(O["qkv_s"][0, :, 2, ds(col, n)], rows[3:11, s0:s0 + n]).then_inc(tails_stored, 16)
                if not last:
                    load_states(grp + 1, grp * 4 + 4)
                pool.wait_ge(g["s2"], grp + 1)
                pool.sem_inc(pool_passed, 1)
                pool.dma_start(O["gdn_p"][0, 0, ds(4 * grp, 4), :, :].rearrange("h k v -> k h v"), S[:, :, :]).then_inc(g["stored"], 16)
                pool.wait_ge(sct_staged, grp + 1)
                pool.sem_inc(pool_passed, 1)
                pool.dma_start(O["sc_p"][0, 0, :, ds(grp * COLS, COLS)], stg2[0:2, :, :].rearrange("p a b -> p (a b)")[:, 0:COLS]).then_inc(sct_stored, 16)
                pool.dma_start(O["sc_s"][0, :, 1, ds(grp * COLS, COLS)], stg2[2:10, :, :].rearrange("p a b -> p (a b)")[:, 0:COLS]).then_inc(sct_stored, 16)
                pool.wait_ge(g["stored"], grp * 16 + 16)
                pool.wait_ge(sct_stored, grp * 32 + 32)
                pool.sem_inc(rows_left, 1)

            load_states(0, None)
            with pool.Fori(0, NG - 1) as grp:
                group(grp, False)
            group(NG - 1, True)
            pool.wait_ge(g["o"], NG + 1)
            pool.wait_ge(g["stored"], 16 * NG)
            pool.wait_ge(tails_stored, 16 * 6 * NG)
            pool.wait_ge(sct_stored, 32 * NG)
            def first_pass(b, c):
                pool.dma_start(chunkS[:, c, :, :], I["state_gdn"][0, b, 16 * c:16 * c + 16, :, :].rearrange("h k v -> k h v")).then_inc(s_in[c], 16)

            first_pass(0, 0)
            first_pass(0, 1)
            with pool.Fori(1, NB) as b:
                for c in range(2):
                    pool.wait_ge(s_used, 2 * b + c - 1)
                    pool.sem_inc(pool_passed, 1)
                    first_pass(b, c)
            pool.wait_ge(d_rows, 1)
            for i in range(2):
                pool.dma_start(dT_d[P * i:P * i + P, :], dTs[:, i, :]).then_inc(d_stored, 16)
            pool.wait_ge(d_stored, 32)
            pool.wait_ge(xlo_ready, XR["mix"] + DT)
            pool.dma_start(h[:, :, :].rearrange("p k t -> p (k t)"), hT_d).then_inc(h_in, 16)
            drows = dT_d.rearrange("(b c j) v -> b c (j v)", b=NB, c=2)

            def load(c, b2, s):
                pool.dma_start(sS[:, s, :, :], I["state_gdn"][0, 2 * b2 + s, 16 * c:16 * c + 16, :, :].rearrange("h k v -> k h v")).then_inc(n_in[s], 16)
                pool.dma_start(sD[:, s, :, :].rearrange("p j v -> p (j v)"),
                               drows[2 * b2 + s, c, :].partition_broadcast(P)).then_inc(n_in[s], 16)

            def store(c, b2, s):
                pool.wait_ge(n_done, b2 * 2 + (8 * c + s + 1))
                pool.sem_inc(pool_passed, 1)
                pool.dma_start(O["gdn_s"][0, 2 * b2 + s, 16 * c:16 * c + 16, :, :].rearrange("h k v -> k h v"), sS[:, s, :, :]).then_inc(n_stored[s], 16)
                pool.wait_ge(n_stored[s], b2 * 16 + (16 * 4 * c + 16))
                pool.sem_inc(pool_passed, 1)

            for s in range(2):
                load(0, 0, s)
            for c in range(2):
                with pool.Fori(0, NB // 2 - 1) as b2:
                    for s in range(2):
                        store(c, b2, s)
                        load(c, b2 + 1, s)
                for s in range(2):
                    store(c, NB // 2 - 1, s)
                    if c == 0:
                        load(1, 0, s)
            pool.dma_start(prow[:, 0, :], I["p_prompt"][0, 0, 0:P, :]).then_inc(p_in, 16)
            pool.dma_start(prow[:, 1, :], I["p_prompt"][0, 0, P:2 * P, :]).then_inc(p_in, 16)
            pool.dma_start(prow[0:NB, 2, :], I["p_sample"][0, :, 0, :]).then_inc(p_in, 16)

        @block.tensor
        def _(pe):
            pe.sem_inc(sc_turned, 1)
            pe.sem_inc(sct_turned, 1)

            def mm(out, lhsT, rhs, start=True, stop=True):
                return pe.matmul(out, lhsT, rhs, start=start, stop=stop)

            def norm_sums(n, tiles=range(DT)):
                for kt in tiles:
                    pe.wait_ge(sq_ready, DT * n + kt + 1)
                    src = sqr if n == 0 else sqh
                    m = mm(bank[4][:, 0:N], ones[:, :], src[:, kt, :], kt == 0, kt == DT - 1)
                if tiles[-1] == DT - 1:
                    m.then_inc(sum_ready, 1)

            def gdn(slot, gr):
                B = bank
                if slot == 0:
                    pe.wait_ge(g["olog"], gr + 1)
                    pe.wait_ge(silu_done, 4 * gr + 4)
                    for i in range(8):
                        m = mm(B[4 + i // 4][0:11, (i % 4) * P:(i % 4 + 1) * P], tail[:, i, 0:11], ident[:, :])
                    m.then_inc(tails_turned, 1)
                elif slot == 1:
                    pe.wait_ge(g["squares"], gr + 1)
                    mm(B[4][:, :], ones[:, :], GW[:, 4, :])
                    mm(B[5][:, :], ones[:, :], GW[:, 9, :]).then_inc(g["sums"], 1)
                elif slot == "decay":
                    pe.wait_ge(g["gsel"], gr + 1)
                    mm(B[6][:, :], ones[0:32, :], GW[0:32, 3, :])
                    mm(B[7][:, :], ones[0:32, :], GW[0:32, 8, :]).then_inc(g["gb"], 1)
                elif slot == 3:
                    pe.wait_ge(g["qkn"], gr + 1)
                    for c in range(NCH):
                        t = slice(c * CH, c * CH + CH)
                        for j in range(2):
                            mm(B[4 + c][:, j * CH:(j + 1) * CH], sqk[:, 2 + j, t], sqk[:, 2 + j, t])
                            m = mm(B[4 + c][:, (2 + j) * CH:(3 + j) * CH], sqk[:, 2 + j, t], sqk[:, j, t])
                    m.then_inc(g["kkqk"], 1)
                    pe.wait_ge(g["dt"], gr + 1)
                    for c in range(NCH):
                        for j in range(2):
                            n = 2 * c + j
                            pe.transpose(B[6][:, n * P:(n + 1) * P], sqk[:, 2 + j, c * CH:c * CH + CH], ident[:, :])
                    for i in range(4):
                        m = pe.transpose(B[7][:, i * P:(i + 1) * P], sv[:, i, 0:CH], ident[:, :])
                    m.then_inc(g["turned"], 1)
                elif slot == 4:
                    pe.wait_ge(g["lt"], gr + 1)
                    for c in range(NCH):
                        for i in range(4):
                            m = pe.transpose(B[4 + c][:, i * P:(i + 1) * P], GW[:, 5 * c + 1, i * CH:(i + 1) * CH], ident[:, :])
                    m.then_inc(g["lt_turned"], 1)
                    pe.wait_ge(g["copied"], gr + 1)
                    for i in range(4):
                        m = pe.transpose(B[6][:, i * P:(i + 1) * P], sv[:, i, CH:2 * CH], ident[:, :])
                    m.then_inc(g["vturned"], 1)
                elif 5 <= slot <= 16 and slot % 2:
                    lv = (slot - 5) // 2 + 1
                    pe.wait_ge(g["x"], LV * gr + lv)
                    for c in range(NCH):
                        for i in range(4):
                            s = slice(i * CH, i * CH + CH)
                            m = mm(B[4 + c][:, s], GW[:, 5 * c + 1, s], GW[:, 5 * c + 3, s])
                    m.then_inc(g["y"], 1)
                elif 5 <= slot <= 16:
                    lv = (slot - 6) // 2 + 1
                    pe.wait_ge(g["ycopied"], (LV - 1) * gr + lv)
                    for c in range(NCH):
                        for i in range(4):
                            s = slice(i * CH, i * CH + CH)
                            if lv < LV - 1:
                                mm(B[4 + c][:, s], GW[:, 5 * c + 4, s], GW[:, 5 * c, s])
                            m = mm(B[6 + c][:, s], GW[:, 5 * c, s], GW[:, 5 * c + 4, s])
                    m.then_inc(g["xy"], 1)
                elif slot == 17:
                    pe.wait_ge(g["x"], LV * gr + LV)
                    for i in range(4):
                        s = slice(i * CH, i * CH + CH)
                        m = mm(B[4][:, s], GW[:, 4, s], vTok[:, 0, i, :])
                    m.then_inc(g["u0"], 1)
                elif slot == 18:
                    pe.wait_ge(g["u0s"], gr + 1)
                    for i in range(4):
                        s = slice(i * CH, i * CH + CH)
                        mm(B[5][:, s], GW[:, 3, s], GW[:, 1, s])
                        m = mm(B[6][:, s], GW[:, 1, s], GW[:, 2, s])
                    m.then_inc(g["s1"], 1)
                elif slot == 19:
                    pe.wait_ge(g["s1c"], gr + 1)
                    for i in range(4):
                        m = mm(B[4][:, i * P:(i + 1) * P], sqk[:, 2 + i // 2, CH:2 * CH], S[:, i, :])
                    m.then_inc(g["ks"], 1)
                elif slot == 20:
                    pe.wait_ge(g["r"], gr + 1)
                    for i in range(4):
                        m = mm(B[5][:, i * P:(i + 1) * P], GW[:, 9, i * CH:(i + 1) * CH], vTok[:, 1, i, :])
                    m.then_inc(g["u1"], 1)
                elif slot == 21:
                    pe.wait_ge(g["u1s"], gr + 1)
                    for i in range(4):
                        s = slice(i * CH, i * CH + CH)
                        mm(B[7][:, s], S[:, i, :], EG[:, i, :], True, False)
                        mm(B[7][:, s], GW[:, 6, s], GW[:, 7, s], False, True)
                        m = mm(B[4][:, s], GW[:, 8, s], GW[:, 6, s])
                    m.then_inc(g["o1"], 1)
                elif slot == 22:
                    pe.wait_ge(g["osq"], gr + 1)
                    mm(B[5][:, :], ones[:, :], GW[:, 4, :])
                    mm(B[6][:, :], ones[:, :], GW[:, 9, :]).then_inc(g["osum"], 1)
                elif slot == 23:
                    pe.wait_ge(sconv_done, gr + 1)
                    for t in range(2):
                        m = mm(B[7][0:10, t * P:(t + 1) * P], tail[:, 8 + t, 0:10], ident[:, :])
                    m.then_inc(sct_turned, 1)

            def extra(ph, it, j):
                gr = group_of(ph, it)
                if gr is not None:
                    for step in PE_STEP.get(j, ()):
                        gdn(step, gr)
                elif ph.name == "first" and j == 9:
                    pe.wait_ge(rows_ready, 1)
                    pe.wait_ge(diag_ready, 1)
                    n = 0
                    for q in (Gc, prep[0:32, 3, :], prep[0:32, 5, :], prep[0:32, 6, :]):
                        for c in range(NCH):
                            src = q[:, c * CH:(c + 1) * CH]
                            pe.transpose(bank[7][:, n * 32:(n + 1) * 32], src, ident[0:32, 0:32])
                            n += 1
                    mm(bank[5][:, :], ones[0:32, :], dgs[:, 0:16, :].rearrange("p a b -> p (a b)"))
                    mm(bank[6][:, 0:32], ones[0:32, :], dgs[:, 16, :]).then_inc(tok_turned, 1)
                elif ph.name == "sb" and j == 1:
                    pe.wait_ge(kq_sq, 1)
                    mm(bank[5][:, 0:256], ones[:, :], sq2[:, 0, :, :].rearrange("p a b -> p (a b)")).then_inc(kq_sum, 1)
                elif ph.name == "sb" and j == 4:
                    pe.wait_ge(kq_prod, 1)
                    mm(bank[6][:, 0:HK * NB], ones[:, :], sq2[:, 0, 0:HK, :].rearrange("p a b -> p (a b)")).then_inc(kq_dot, 1)
                elif ph.name == "gates" and j % 4 == 3:
                    c = j // 4
                    pe.wait_ge(s_in[c], 16 * (it + 1))
                    for i in range(16):
                        m = mm(bank[4][:, ds(it * 64 + 32 * c + 2 * i, 2)], chunkS[:, c, i, :],
                               kqs[:, 8 * c + i // 2, ds(it, 1), :].rearrange("p a b -> p (a b)"))
                    m.then_inc(s_used, 1)
                elif ph.name == "yb0" and j == 2:
                    pe.wait_ge(d_ready, 1)
                    for i in range(2):
                        m = pe.transpose(bank[5][:, i * P:(i + 1) * P], so[:, 0, :, :].rearrange("p a b -> p (a b)")[:, i * P:(i + 1) * P], ident[:, :])
                    m.then_inc(d_turned, 1)
                elif ph.name in NORM and j < 4:
                    norm_sums(NORM[ph.name], range(4 * j, 4 * j + 4))
                elif ph.name == "pgate_last" and j < 7:
                    norm_sums(3, range(2 * j, 2 * j + 2))
                elif ph.name == "yb0" and j == 4:
                    pe.wait_ge(so_sq, 1)
                    mm(bank[7][:, 0:256], ones[:, :], so[:, 3, :, :].rearrange("p a b -> p (a b)")).then_inc(so_sum, 1)

            def turn_states(q, ph, it, par):
                if q.kind == "qkv":
                    kind, p, gx = q.arg
                    i = {"v": p, "q": 2, "k": 3}[kind]
                    pe.wait_ge(st_in[i % 2], 32 * gx(it) + 16 * (i // 2 + 1))
                    for t in range(2):
                        m = mm(bank[2 * par + t][:, N:N + 24], st_qkv[:, i % 2, t, :], ident[0:24, 0:24])
                    m.then_inc(st_turned, 1)
                elif q.kind == "sh":
                    pe.wait_ge(sc_in, 16 * (q.arg(it) + 1))
                    for t in range(2):
                        m = mm(bank[2 * par + t][:, N:N + 16], st_sc[:, t, :], ident[0:16, 0:16])
                    m.then_inc(sc_turned, 1)

            def body(ph, it):
                j = 0
                for qi, q in enumerate(ph.pairs):
                    n = ph.q0 + qi
                    par = n % 2
                    if n >= 2:
                        pe.wait_ge(pair_free[par], it * (len(ph.pairs) // 2) + n // 2)
                    turn_states(q, ph, it, par)
                    kt, last = 0, sum(q.kts) - 1
                    for m_ in q.kts:
                        if q.rhs[0] is ahi:
                            pe.wait_ge(a_ready, FP * int(q.xready[3:]) + (kt + m_ + 1) // 2)
                        else:
                            pe.wait_ge(xlo_ready, XR[q.xready] + kt + m_)
                        pe.wait_ge(lo_ready, piece(ph, it, j))
                        sl = (ph.p0 + j) % SPLIT
                        for t in range(q.tiles):
                            for k in range(m_):
                                out = bank[2 * par + t][:, 0:N]
                                w = (whi[:, sl, k, t * P:(t + 1) * P], wlo[:, sl, k, t * P:(t + 1) * P])
                                mm(out, w[0], q.rhs[0][:, kt + k, :], kt + k == 0, False)
                                mm(out, w[0], q.rhs[1][:, kt + k, :], False, False)
                                m = mm(out, w[1], q.rhs[0][:, kt + k, :], False, kt + k == last)
                        m.then_inc(piece_used, 1)
                        kt += m_
                        extra(ph, it, j)
                        j += 1

            def work(when, ph, it):
                if when == "body":
                    return body(ph, it)
                if ph.name == "first":
                    pe.wait_ge(ident_ready, 1)
                    pe.wait_ge(v_in, 16 * 8)
                    for i in range(3):
                        r = 113 if i == 2 else P
                        m = pe.transpose(bank[i][:, 0:r], vrow[0:r, i, :], ident[0:r, 0:r])
                    m.then_inc(vec_turned, 1)
                    pe.wait_ge(vec_ready, 1)
                    pe.wait_ge(x_in, 16 * (BLK + 1))
                    for kt in range(DT):
                        if kt >= 8:
                            pe.wait_ge(h_copied, kt - 7)
                        for b in range(BLK):
                            pe.transpose(bank[kt % 8][:, b * P:(b + 1) * P], xrow[:, b, kt * P:(kt + 1) * P], ident[:, :])
                        pe.transpose(bank[kt % 8][:, T:N], xrow[0:NB, BLK, kt * P:(kt + 1) * P], ident[0:NB, 0:NB]).then_inc(x_turned, 1)
                elif ph.name == "pproj":
                    pe.wait_ge(p_in, 16 * (BLK + 1))
                    for k in range(PD // P):
                        for b in range(BLK):
                            pe.transpose(bank[5 + k][:, b * P:(b + 1) * P], prow[:, b, k * P:(k + 1) * P], ident[:, :])
                        m = pe.transpose(bank[5 + k][:, T:N], prow[0:NB, BLK, k * P:(k + 1) * P], ident[0:NB, 0:NB])
                    m.then_inc(p_turned, 1)

            walk(pe, work)
            norm_sums(3, range(DT - 2, DT))
            n = 0
            for b in range(BLK + 1):
                r = P if b < BLK else NB
                for k4 in range(DT // 4):
                    pe.wait_ge(y_ready, 4 * k4 + 4)
                    if n >= 4:
                        pe.wait_ge(y_copied, n - 3)
                    for k in range(4):
                        m = pe.transpose(bank[n % 4][0:r, k * P:(k + 1) * P], h[:, 4 * k4 + k, b * P:b * P + r], ident[:, :])
                    m.then_inc(y_turned, 1)
                    n += 1

        @block.scalar
        def _(act):
            mine = Count(act_self)
            act.sem_inc(g["olog"], 1)
            vw = I["qkv_conv_w"][0].rearrange("j (t p) -> (j t) p", p=P)
            act.dma_start(vrow[:, 0, :], vw[0:P]).then_inc(v_in, 16)
            act.dma_start(vrow[:, 1, :], vw[P:2 * P]).then_inc(v_in, 16)
            act.dma_start(vrow[0:48, 2, :], I["sconv_w"][0].rearrange("j (t p) -> (j t) p", p=P)).then_inc(v_in, 16)
            for n, name in enumerate(("attn_norm", "ffn_norm", "ple_norm")):
                act.dma_start(vrow[48 + 16 * n:64 + 16 * n, 2, :], I[name][0].rearrange("(t p) -> t p", p=P)).then_inc(v_in, 16)
            act.dma_start(vrow[96:112, 2, :], I["final_norm"].rearrange("(t p) -> t p", p=P)).then_inc(v_in, 16)
            act.dma_start(vrow[112:113, 2, :], I["gdn_norm"]).then_inc(v_in, 16)
            with nc.allow_non_contiguous_dma(reason="32 values each, once"):
                act.dma_start(prep[0:HV, 10, 0:1], I["a_log"].rearrange("o h -> h o")).then_inc(col_in, 16)
                act.dma_start(prep[0:HV, 10, 1:2], I["dt_bias"].rearrange("o h -> h o")).then_inc(col_in, 16)

            def split(n, at_, cnt):
                act.wait_ge(raw_loaded[at_ % RAW], n)
                if at_ >= SPLIT:
                    act.wait_ge(piece_used, cnt - SPLIT)
                act.activation(whi[:, at_ % SPLIT, :, :], raw[:, at_ % RAW, :, :], ACT.Copy).then_inc(hi_ready, 1)

            def split_ahead(ph, it, j):
                at_ = ph.p0 + j + AHEAD
                if ph.iters == 1 and at_ >= PIECES:
                    return
                split(it * (ph.pieces // RAW * 16) + 16 * (at_ // RAW + 1), at_, it * ph.pieces + at_ + 1)

            def squares(src, dst, tiles):
                for kt in tiles:
                    act.activation(dst[:, kt, :], src[:, kt, :], ACT.Square).then_inc(sq_ready, 1)

            def scaled_hi(gain):
                for kt in range(DT):
                    act.activation(xhi[:, kt, :], h[:, kt, :], ACT.Copy, scale=vec[:, gain + kt:gain + kt + 1]).then_inc(xhi_ready, 1)

            def plain_split(src, p0=None):
                for kt in range(DT):
                    if p0 is not None and kt % KT == 0:
                        act.wait_ge(piece_used, p0 - 3 + kt // KT)
                    act.activation(xhi[:, kt, :], src(kt), ACT.Copy).then_inc(xhi_ready, 1)

            def gdn(slot, gr):
                if slot == 0:
                    act.wait_ge(tails_turned, gr + 1)
                    rows = stg[:, :, :, :].rearrange("p a b c -> p (a b c)")
                    for i in range(2):
                        m = act.activation(rows[0:11, i * 512:(i + 1) * 512], bank[4 + i][0:11, :], ACT.Copy)
                    m.then_inc(tails_staged, 1)
                    act.wait_ge(silu_done, 4 * gr + 4)
                    act.wait_ge(g["o"], gr + 1)
                    act.activation(GW[:, 4::5, :].rearrange("p a (b t) -> p a b t", b=2),
                                   sqk[:, :, 0:T].rearrange("p (a b) t -> p a b t", b=2), ACT.Square).then_inc(g["squares"], 1)
                elif slot == 1:
                    act.wait_ge(g["sums"], gr + 1)
                    act.activation(GW[:, 4, :], bank[4][:, :], ACT.Ln, bias=eps[:, :])
                    act.activation(GW[:, 9, :], bank[5][:, :], ACT.Ln, bias=eps[:, :]).then_inc(g["log"], 1)
                    act.wait_ge(g["log"], gr + 1)
                    act.activation(GW[:, 4::5, :], GW[:, 4::5, :], ACT.Exp, scale=-0.5).then_inc(g["root"], 1)
                elif slot == 2:
                    act.wait_ge(g["expo"], gr + 1)
                    act.activation(EG[:, :, :].rearrange("p a b -> p (a b)"), bank[7][:, :], ACT.Exp)
                    act.activation(GW[:, 0::5, :], GW[:, 0::5, :], ACT.Exp).then_inc(g["dt"], 1)
                elif slot == 3:
                    act.wait_ge(g["turned"], gr + 1)
                    act.wait_ge(tails_stored, 96 * (gr + 1))
                    act.activation(kTok[:, :, :, :].rearrange("p a b c -> p (a b c)"), bank[6][:, :], ACT.Copy)
                    act.activation(vTok[:, 0, :, :].rearrange("p b c -> p (b c)"), bank[7][:, :], ACT.Copy).then_inc(g["copied"], 1)
                    I4 = ident[:, :].unsqueeze(1).to_broadcast([P, 4, P])
                    for n in (3, 8, 4, 9):
                        m = act.activation(GW[:, n, :].rearrange("p (a b) -> p a b", a=4), I4, ACT.Copy)
                    m.then_inc(g["xinit"], 1)
                elif slot == 4:
                    act.wait_ge(g["vturned"], gr + 1)
                    act.activation(vTok[:, 1, :, :].rearrange("p b c -> p (b c)"), bank[6][:, :], ACT.Copy)
                elif 5 <= slot <= 16 and slot % 2:
                    lv = (slot - 5) // 2 + 1
                    act.wait_ge(g["y"], (LV - 1) * gr + lv)
                    act.activation(half(GW[:, 0, :], lv, 0), half(bank[4][:, :], lv, 0), ACT.Copy)
                    act.activation(half(GW[:, 5, :], lv, 0), half(bank[5][:, :], lv, 0), ACT.Copy).then_inc(g["ycopied"], 1)
                elif slot == 18:
                    act.wait_ge(g["s1"], gr + 1)
                    act.wait_ge(rows_left, gr + 1)
                    act.activation(S[:, :, :].rearrange("p a b -> p (a b)"), bank[5][:, :], ACT.Copy).then_inc(g["s1c"], 1)
                    act.activation(GW[:, 0, :], bank[6][:, :], ACT.Copy)
                    act.activation(GW[:, 4, :], bank[6][:, :], ACT.Square)
                elif slot == 21:
                    act.wait_ge(g["o1"], gr + 1)
                    act.activation(GW[:, 5, :], bank[7][:, :], ACT.Copy)
                    act.activation(GW[:, 9, :], bank[7][:, :], ACT.Square).then_inc(g["osq"], 1)
                elif slot == 22:
                    act.wait_ge(g["osum"], gr + 1)
                    act.activation(GW[:, 4, :], bank[5][:, :], ACT.Ln, scale=1.0 / P, bias=eps[:, :])
                    act.activation(GW[:, 9, :], bank[6][:, :], ACT.Ln, scale=1.0 / P, bias=eps[:, :]).then_inc(g["olog"], 1)
                    act.wait_ge(g["olog"], gr + 2)
                    act.activation(GW[:, 4::5, :], GW[:, 4::5, :], ACT.Exp, scale=-0.5).then_inc(g["oroot"], 1)
                elif slot == 23:
                    act.wait_ge(sct_turned, gr + 2)
                    act.wait_ge(rows_left, gr + 1)
                    act.activation(stg2[0:10, :, :].rearrange("p a b -> p (a b)")[:, 0:COLS], bank[7][0:10, 0:2 * P], ACT.Copy).then_inc(sct_staged, 1)

            def evac(q, ph, it, qi):
                n = ph.q0 + qi
                par = n % 2
                bk = bank[2 * par], bank[2 * par + 1]
                free = lambda m: m.then_inc(pair_free[par], 1)
                if q.kind == "ab":
                    freed(act, ph, it, qi)
                    R = slice(0, 32)
                    mine.inc(act.activation(prep[R, 3, :], prep[32:64, 0, :], ACT.Sigmoid))
                    act.wait_ge(col_in, 32)
                    act.activation(prep[R, 10, 3:4], prep[R, 10, 0:1], ACT.Exp).then_inc(ea_ready, 1)
                    act.wait_ge(soft_in, 1)
                    mine.inc(act.activation(prep[R, 2, :], prep[R, 1, :], ACT.Abs))
                    mine.settle(act)
                    mine.inc(act.activation(prep[R, 2, :], prep[R, 2, :], ACT.Exp, scale=-1.0))
                    mine.settle(act)
                    act.activation(prep[R, 2, :], prep[R, 2, :], ACT.Ln, bias=1.0).then_inc(soft_ready, 1)
                    act.wait_ge(g_ready, 1)
                    act.activation(prep[R, 8, 0:NB], prep[R, 4, T:N], ACT.Exp)
                    act.activation(prep[R, 5, 0:T], Gc[:, :], ACT.Exp)
                    for c in range(NCH):
                        m = act.activation(prep[R, 6, c * CH:(c + 1) * CH], Gc[:, c * CH:(c + 1) * CH], ACT.Exp,
                                           scale=-1.0, bias=Gc[:, (c + 1) * CH - 1:(c + 1) * CH])
                    m.then_inc(rows_ready, 1)
                elif q.kind == "z":
                    p, gx = q.arg
                    if ph.name == "first":
                        act.wait_ge(h_stored, 16)
                    act.wait_ge(z_scaled, gx(it) * 2 + p + 1)
                    for t in range(2):
                        m = act.activation(o_all[:, ds(gx(it) * 4 + 2 * p + t, 1), :].rearrange("p a b -> p (a b)"), bk[t][:, 0:N], ACT.Silu)
                    free(m)
                elif q.kind == "qkv":
                    kind, p, gx = q.arg
                    i = {"v": p, "q": 2, "k": 3}[kind[0]]
                    act.wait_ge(conv_done, gx(it) * 4 + i + 1)
                    if ph.name == "first" and kind == "q":
                        act.wait_ge(tok_turned, 1)
                    for t in range(2):
                        dst = sv[:, 2 * p + t, 0:T] if kind == "v" else sqk[:, {"q": 0, "k": 2}[kind] + t, 0:T]
                        tile = {"q": gx(it) * 2 + t, "k": gx(it) * 2 + HK + t, "v": gx(it) * 4 + 2 * HK + 2 * p + t}[kind]
                        act.activation(dst, cacc[:, t, 0:T], ACT.Silu)
                        m = act.activation(smp[:, ds(tile, 1), :].rearrange("p a b -> p (a b)"), cacc[:, t, T + 3::4], ACT.Silu)
                    m.then_inc(silu_done, 1)
                elif q.kind == "sh":
                    act.wait_ge(sconv_done, q.arg(it) + 1)
                    for t in range(2):
                        row = yb[:, ds(q.arg(it) * 2 + t, 1), :].rearrange("p a b -> p (a b)")
                        act.activation(row[:, 0:T], cacc[:, t, 0:T], ACT.Copy)
                        m = act.activation(row[:, T:N], cacc[:, t, T + 3::4], ACT.Copy)
                    m.then_inc(yb_ready, 1)
                elif q.kind == "gate":
                    dst = (sgA, sgB)[qi]
                    act.wait_ge(gate_scaled, it * 2 + qi + 1)
                    for t in range(2):
                        m = act.activation(dst[:, ds(it * 2 + t, 1), :].rearrange("p a b -> p (a b)"), bk[t][:, 0:N], ACT.Sigmoid)
                    free(m)
                elif q.kind == "fg":
                    ax, half, r = q.arg
                    act.wait_ge(fg_scaled, ax(it) + (half * FP + r + 1))
                    for t in range(2):
                        m = act.activation(et[:, t, :], bk[t][:, 0:N], ACT.Silu)
                    free(m)
                elif q.kind == "fu":
                    ax, half, r = q.arg
                    freed(act, ph, it, qi)
                    for t in range(2):
                        m = act.activation(ahi[:, ds((ax(it) + r) * 2 + t, 1), :], et[:, 2 + t, :].unsqueeze(1), ACT.Copy)
                    m.then_inc(a_hi, 1)
                elif q.kind == "pp":
                    act.wait_ge(piece_used, piece(ph, it, qi))
                    for t in range(2):
                        m = act.activation(pp[:, 2 * q.arg(it) + t, :], bk[t][:, 0:N], ACT.Copy)
                    free(m)
                elif q.kind == "pg":
                    act.wait_ge(pg_scaled, q.arg(it) + 1)
                    for t in range(2):
                        m = act.activation(et[:, t, :], bk[t][:, 0:N], ACT.Sigmoid)
                    m.then_inc(pg_done, 1)

            def extra(ph, it, j):
                gr = group_of(ph, it)
                if gr is not None:
                    for step in ACT_STEP.get(j, ()):
                        gdn(step, gr)
                elif ph.name == "pgate_last" and j < 7:
                    if j == 0:
                        freed_all(act, by["pgate"])
                    elif j == 6:
                        freed(act, ph, it, 0)
                    squares(h, sqh, range(2 * j, 2 * j + 2))
                elif ph.name in NORM and j < 4:
                    squares(*((hpro, sqr) if ph.name == "first" else (h, sqh)), range(4 * j, 4 * j + 4))
                    if j == 3:
                        act.wait_ge(mean_ready, NORM[ph.name] + 1)
                        act.activation(rstd[:, :], rstd[:, :], ACT.Sqrt).then_inc(rstd_ready, 1)
                elif ph.name == "sb" and j == 0:
                    act.wait_ge(g["o"], NG + 1)
                    act.activation(sq2[:, 0, :, :], smp[:, 0:2 * HK, :], ACT.Square).then_inc(kq_sq, 1)
                elif ph.name == "sb" and j == 2:
                    act.wait_ge(kq_rec, 1)
                    act.activation(sq2[:, 1, :, :], sq2[:, 1, :, :], ACT.Sqrt).then_inc(kq_root, 1)
                elif ph.name == "yb0" and j == 2:
                    act.wait_ge(d_turned, 1)
                    act.activation(dTs[:, :, :].rearrange("p a b -> p (a b)"), bank[5][:, 0:2 * P], ACT.Copy).then_inc(d_rows, 1)
                    act.activation(so[:, 3, :, :], so[:, 2, :, :], ACT.Square).then_inc(so_sq, 1)
                elif ph.name == "yb0" and j == 5:
                    act.wait_ge(so_rec, 1)
                    act.activation(so[:, 4, :, :], so[:, 4, :, :], ACT.Sqrt).then_inc(so_root, 1)
                elif ph.name in ("ffn0s", "ffn1s") and j % 8 in (2, 3, 4, 5):
                    s, c, quarter = j // 8, int(ph.name[3]), j % 8 - 2
                    if quarter == 0:
                        act.wait_ge(n_in[s], it * 32 + (128 * c + 32))
                    for i in range(4 * quarter, 4 * quarter + 4):
                        m = act.activation(sS[:, s, i, :], sS[:, s, i, :], ACT.Copy,
                                           scale=bc[:, ds(it * 2 + (s + 1), 1), 16 * c + i:16 * c + i + 1].rearrange("p a b -> p (a b)"))
                    m.then_inc(n_scaled, 1)

            def work(when, ph, it):
                if when == "body":
                    j, late = 0, None
                    for qi, q in enumerate(ph.pairs):
                        for n in range(len(q.kts)):
                            split_ahead(ph, it, j)
                            extra(ph, it, j)
                            if late is not None and n == 1:
                                evac(ph.pairs[late], ph, it, late)
                                late = None
                            j += 1
                        if q.kind in ("qkv", "sh") and qi + 1 < len(ph.pairs):
                            late = qi
                        else:
                            evac(q, ph, it, qi)
                    return
                name = ph.name
                if name == "first":
                    act.wait_ge(vec_ready, 1)
                    for kt in range(DT):
                        act.wait_ge(h_copied, kt + 1)
                        act.activation(xhi[:, kt, :], hpro[:, kt, :], ACT.Copy, scale=vec[:, 304 + kt:305 + kt]).then_inc(xhi_ready, 1)
                    for p in range(AHEAD):
                        split(16, p, p + 1)
                elif name == "gates":
                    act.wait_ge(kq_dot, 1)
                    act.wait_ge(kq_ready, 1)
                elif name == "yb0":
                    freed_all(act, by["sb"])
                    plain_split(lambda kt: yb[:, kt, :], ph.p0)
                elif name == "ya0":
                    act.wait_ge(so_done, 1)
                    plain_split(lambda kt: o_all[:, kt, :], ph.p0)
                elif name == "ya1":
                    plain_split(lambda kt: o_all[:, DT + kt, :], ph.p0)
                elif name == "wo":
                    act.wait_ge(piece_used, ph.p0)
                    freed_all(act, by["ya1"])
                    plain_split(lambda kt: sgB[:, kt, :])
                elif name == "ffn0r":
                    act.wait_ge(piece_used, ph.p0)
                    freed_all(act, by["wo"])
                    scaled_hi(320)
                elif name == "ffn1r":
                    act.wait_ge(piece_used, ph.p0)
                elif name == "pproj":
                    act.wait_ge(p_turned, 1)
                    for k in range(PD // P):
                        act.activation(phi[:, k, :], bank[5 + k][:, 0:N], ACT.Copy).then_inc(xhi_ready, 1)
                elif name == "pgate_first":
                    freed_all(act, by["down1"])
                    scaled_hi(336)

            walk(act, work)
            freed_all(act, by["pgate_last"])
            squares(h, sqh, range(DT - 2, DT))
            act.wait_ge(mean_ready, 4)
            act.activation(rstd[:, :], rstd[:, :], ACT.Sqrt).then_inc(rstd_ready, 1)
            n = 0
            for b in range(BLK + 1):
                r = P if b < BLK else NB
                for k4 in range(DT // 4):
                    act.wait_ge(y_turned, n + 1)
                    act.activation(yrow[0:r, b, k4 * 512:(k4 + 1) * 512], bank[n % 4][0:r, :], ACT.Copy).then_inc(y_copied, 1)
                    n += 1

        @block.vector
        def _(dve):
            mine = Count(dve_self)
            dve.sem_inc(g["o"], 1)
            dve_per = {"groups": 17, "gates": 0, "yb1": 0, "ya0": 2, "ya1": 2, "wo": 0,
                       "ffn0s": 2, "ffn1s": 2, "down0": 0, "down1": 0, "pgate": 2}
            f32 = lambda v: v.bitcast(F32)

            def split(at_, cnt):
                dve.wait_ge(hi_ready, cnt)
                dve.tensor_tensor(wlo[:, at_ % SPLIT, :, :], raw[:, at_ % RAW, :, :], f32(whi[:, at_ % SPLIT, :, :]),
                                  ALU.subtract).then_inc(lo_ready, 1)

            def split_ahead(ph, it, j):
                at_ = ph.p0 + j + AHEAD
                if ph.iters == 1 and at_ >= PIECES:
                    return
                split(at_, it * ph.pieces + at_ + 1)

            def norm_split(xr, gain, psum=False):
                def copy(kt):
                    dve.wait_ge(x_turned, kt + 1)
                    dve.tensor_copy(hpro[:, kt, :], bank[kt % 8][:, 0:N]).then_inc(h_copied, 1)

                if psum:
                    copy(0)
                for kt in range(DT):
                    if psum and kt + 1 < DT:
                        copy(kt + 1)
                    dve.wait_ge(xhi_ready, xr + kt + 1)
                    dve.scalar_tensor_tensor(out=xlo[:, kt, :], in0=(hpro if psum else h)[:, kt, :],
                                             scalar=vec[:, gain + kt:gain + kt + 1], in1=f32(xhi[:, kt, :]),
                                             op0=ALU.mult, op1=ALU.subtract).then_inc(xlo_ready, 1)

            def plain_split(xr, src, n=DT, dst=(xhi, xlo)):
                for kt in range(n):
                    dve.wait_ge(xhi_ready, xr + kt + 1)
                    dve.tensor_tensor(dst[1][:, kt, :], src(kt), f32(dst[0][:, kt, :]), ALU.subtract).then_inc(xlo_ready, 1)

            def norm_mean(n):
                dve.wait_ge(sum_ready, n + 1)
                mine.inc(dve.tensor_scalar(rstd[:, :], bank[4][:, 0:N], 1.0 / D, EPS, ALU.mult, ALU.add))
                mine.settle(dve)
                dve.reciprocal(rstd[:, :], rstd[:, :]).then_inc(mean_ready, 1)
                dve.wait_ge(rstd_ready, n + 1)

            def col(t, *i):
                v = t[(slice(None), *i[:-1], ds(i[-1], 1))]
                return v

            def gdn(slot, gr):
                hd = lambda i: gr * 4 + i
                H4 = lambda n: GW[:, n, :].rearrange("p (a b) -> p a b", a=4)
                if slot == "decay":
                    Gv = Gc[:, :].rearrange("p (c t) -> p c t", c=NCH)
                    for i in range(4):
                        m = dve.tensor_scalar(GW[0:32, 3::5, i * CH:(i + 1) * CH], Gv, ident[0:32, ds(hd(i), 1)], None, ALU.mult)
                    m.then_inc(g["gsel"], 1)
                elif slot == "exponents":
                    dve.wait_ge(g["gb"], gr + 1)
                    for c in range(NCH):
                        for i in range(4):
                            s = slice(i * CH, i * CH + CH)
                            m = dve.scalar_tensor_tensor(out=GW[:, 5 * c, s], in0=bank[6 + c][:, s], scalar=col(tok, 0, c, hd(i)),
                                                         in1=later[:, :], op0=ALU.subtract, op1=ALU.add)
                    m.then_inc(g["expo"], 1)
                elif slot == 2:
                    dve.wait_ge(g["root"], gr + 1)
                    dve.scalar_tensor_tensor(out=sqk[:, 0:2, 0:T], in0=sqk[:, 0:2, 0:T], scalar=QSCALE,
                                             in1=GW[:, 4, :].rearrange("p (a t) -> p a t", a=2), op0=ALU.mult, op1=ALU.mult)
                    mine.inc(dve.tensor_tensor(sqk[:, 2:4, 0:T], sqk[:, 2:4, 0:T], GW[:, 9, :].rearrange("p (a t) -> p a t", a=2), ALU.mult))
                    dve.wait_ge(g["dt"], gr + 1)
                    mine.settle(dve)
                    for j in range(2):
                        m = dve.tensor_tensor(EG[:, 2 * j:2 * j + 2, :], EG[:, 2 * j:2 * j + 2, :],
                                              sqk[:, j, CH:2 * CH].unsqueeze(1).to_broadcast([P, 2, CH]), ALU.mult)
                    m.then_inc(g["qkn"], 1)
                elif slot == 3:
                    dve.wait_ge(g["kkqk"], gr + 1)
                    for c in range(NCH):
                        for i in range(4):
                            s = slice(i * CH, i * CH + CH)
                            dve.scalar_tensor_tensor(out=GW[:, 5 * c + 1, s], in0=bank[4 + c][:, (i // 2) * CH:(i // 2 + 1) * CH],
                                                     scalar=col(tok, 2, c, hd(i)), in1=GW[:, 5 * c, s], op0=ALU.mult, op1=ALU.mult)
                        for j in range(2):
                            m = dve.tensor_tensor(H4(5 * c + 2)[:, 2 * j:2 * j + 2, :],
                                                  bank[4 + c][:, (2 + j) * CH:(3 + j) * CH].unsqueeze(1).to_broadcast([P, 2, CH]),
                                                  H4(5 * c)[:, 2 * j:2 * j + 2, :], ALU.mult)
                    m.then_inc(g["lt"], 1)
                elif slot == 4:
                    dve.wait_ge(g["xinit"], gr + 1)
                    dve.wait_ge(g["lt"], gr + 1)
                    dve.sem_inc(dve_passed, 1)
                    M = lambda m, lv: m[:, lv, :].unsqueeze(1).to_broadcast([P, 4, CH])
                    for c in range(NCH):
                        dve.copy_predicated(H4(5 * c + 4), M(joinT, 0), H4(5 * c + 1))
                    dve.wait_ge(g["lt_turned"], gr + 1)
                    dve.sem_inc(dve_passed, 1)
                    for c in range(NCH):
                        m = dve.copy_predicated(H4(5 * c + 3), M(join, 0), bank[4 + c][:, :].rearrange("p (a b) -> p a b", a=4))
                    m.then_inc(g["x"], 1)
                elif slot in range(6, 17, 2):
                    lv = (slot - 6) // 2 + 1
                    w = 1 << lv

                    def M(m, side):
                        v = m[:, lv, :].rearrange("p (b t) -> p b t", t=2 * w)[:, :, side * w:(side + 1) * w]
                        return v.unsqueeze(1).to_broadcast([P, 4, CH // (2 * w), w])

                    def V(v, side):
                        return v.rearrange("p (a b t) -> p a b t", a=4, t=2 * w)[:, :, :, side * w:(side + 1) * w]
                    dve.wait_ge(g["xy"], gr * (LV - 1) + lv)
                    dve.sem_inc(dve_passed, 1)
                    for c in range(NCH):
                        if lv < LV - 1:
                            dve.copy_predicated(V(GW[:, 5 * c + 3, :], 0), M(join, 0), V(bank[4 + c][:, :], 0))
                        m = dve.copy_predicated(V(GW[:, 5 * c + 4, :], 1), M(joinT, 1), V(bank[6 + c][:, :], 1))
                    m.then_inc(g["x"], 1)
                elif slot == 17:
                    for c in range(NCH):
                        for i in range(4):
                            dve.tensor_scalar(GW[:, 5 * c + 3, i * CH:(i + 1) * CH], kTok[:, c, i // 2, :], col(tok, 4, c, hd(i)), None, ALU.mult)
                    dve.wait_ge(g["u0"], gr + 1)
                    for i in range(4):
                        s = slice(i * CH, i * CH + CH)
                        m = dve.tensor_scalar(GW[:, 1, s], bank[4][:, s], col(tok, 1, 0, hd(i)), None, ALU.mult)
                    m.then_inc(g["u0s"], 1)
                elif slot == 19:
                    dve.wait_ge(g["ks"], gr + 1)
                    for i in range(4):
                        m = dve.scalar_tensor_tensor(out=vTok[:, 1, i, :], in0=bank[4][:, i * P:(i + 1) * P], scalar=col(tok, 3, 1, hd(i)),
                                                     in1=vTok[:, 1, i, :], op0=ALU.mult, op1=ALU.add)
                    m.then_inc(g["r"], 1)
                elif slot == 20:
                    dve.wait_ge(g["u1"], gr + 1)
                    for i in range(4):
                        s = slice(i * CH, i * CH + CH)
                        m = dve.tensor_scalar(GW[:, 6, s], bank[5][:, s], col(tok, 1, 1, hd(i)), None, ALU.mult)
                    m.then_inc(g["u1s"], 1)
                elif slot == 21:
                    dve.wait_ge(g["o1"], gr + 1)
                    for i in range(4):
                        m = dve.scalar_tensor_tensor(out=S[:, i, :], in0=S[:, i, :], scalar=col(bc, 0, hd(i)),
                                                     in1=bank[4][:, i * P:(i + 1) * P], op0=ALU.mult, op1=ALU.add)
                    m.then_inc(g["s2"], 1)
                elif slot == 23:
                    dve.wait_ge(g["oroot"], gr + 1)
                    mine.inc(dve.scalar_tensor_tensor(out=GW[:, 0::5, :], in0=GW[:, 0::5, :], scalar=vec[:, 368:369],
                                                      in1=GW[:, 4::5, :], op0=ALU.mult, op1=ALU.mult))
                    mine.settle(dve)
                    for c in range(NCH):
                        o = o_all[:, ds(gr * 4, 4), c * CH:(c + 1) * CH]
                        m = dve.tensor_tensor(o, o, H4(5 * c), ALU.mult)
                    m.then_inc(g["o"], 1)

            def conv(first, taps, wcol, done):
                for j in range(taps):
                    for t in range(2):
                        x = cin[:, t, first + j:first + j + 288]
                        w = vec[:, ds(wcol(j, t), 1)]
                        if j == 0:
                            m = dve.tensor_scalar(cacc[:, t, :], x, w, None, ALU.mult)
                        else:
                            m = dve.scalar_tensor_tensor(out=cacc[:, t, :], in0=x, scalar=w, in1=cacc[:, t, :], op0=ALU.mult, op1=ALU.add)
                        if t == 0 and j == taps - 1:
                            continue
                        if t == 1:
                            if j < taps - 1:
                                mine.inc(m)
                                mine.settle(dve)
                            else:
                                m.then_inc(done, 1)

            def evac(q, ph, it, qi, j):
                n = ph.q0 + qi
                par = n % 2
                bk = bank[2 * par], bank[2 * par + 1]
                free = lambda m: m.then_inc(pair_free[par], 1)
                dve.wait_ge(piece_used, piece(ph, it, j - 1)) if q.kind != "pp" else None
                B = [b[:, 0:N] for b in bk]
                if q.kind == "ab":
                    R = slice(0, 32)
                    free(dve.tensor_tensor(prep[0:64, 0, :], bk[0][0:64, 0:N], rstd[0:64, :], ALU.mult))
                    dve.wait_ge(pair_free[0], 1)
                    dve.wait_ge(col_in, 32)
                    dve.tensor_scalar(prep[R, 1, :], prep[R, 0, :], prep[R, 10, 1:2], None, ALU.add).then_inc(soft_in, 1)
                    dve.wait_ge(soft_ready, 1)
                    mine.inc(dve.tensor_scalar(prep[R, 1, :], prep[R, 1, :], 0.0, None, ALU.max))
                    mine.inc(dve.memset(prep[R, 7, :], 1.0))
                    dve.wait_ge(ea_ready, 1)
                    mine.inc(dve.tensor_scalar(prep[R, 10, 2:3], prep[R, 10, 3:4], -1.0, None, ALU.mult))
                    mine.settle(dve)
                    mine.inc(dve.tensor_tensor(prep[R, 1, :], prep[R, 1, :], prep[R, 2, :], ALU.add))
                    mine.settle(dve)
                    mine.inc(dve.tensor_scalar(prep[R, 4, :], prep[R, 1, :], prep[R, 10, 2:3], None, ALU.mult))
                    mine.settle(dve)
                    for c in range(NCH):
                        t = slice(c * CH, (c + 1) * CH)
                        m = dve.tensor_tensor_scan(Gc[:, t], prep[R, 7, t], prep[R, 4, t], 0.0, ALU.mult, ALU.add)
                    m.then_inc(g_ready, 1)
                    dve.wait_ge(rows_ready, 1)
                    I32 = ident[R, 0:32]
                    dve.tensor_scalar(dgs[:, 0, :], I32, prep[R, 5, T - 1:T], None, ALU.mult)
                    for b in range(NB):
                        dve.tensor_scalar(dgs[:, 1 + b, :], I32, prep[R, 8, b:b + 1], None, ALU.mult)
                        m = dve.tensor_scalar(dgs[:, 1 + NB + b, :], I32, prep[R, 3, T + b:T + b + 1], None, ALU.mult)
                    m.then_inc(diag_ready, 1)
                elif q.kind == "z":
                    for t in range(2):
                        m = dve.tensor_tensor(B[t], B[t], rstd[:, :], ALU.mult)
                    m.then_inc(z_scaled, 1)
                elif q.kind == "qkv":
                    kind, p, gx = q.arg
                    i = {"v": p, "q": 2, "k": 3}[kind]
                    first_tile = {"q": gx(it) * 2, "k": gx(it) * 2 + HK, "v": gx(it) * 4 + 2 * HK + 2 * p}[kind]
                    ti = {"v": 2 * p, "q": 4, "k": 6}[kind]
                    if ph.name != "first":
                        dve.wait_ge(tails_turned, gx(it))
                        dve.wait_ge(silu_done, gx(it) * 4 + i)
                        if i == 0:
                            dve.wait_ge(yb_ready, gx(it))
                    elif i:
                        dve.wait_ge(silu_done, i)
                    for t in range(2):
                        dve.tensor_tensor(cin[:, t, 3:3 + T], B[t][:, 0:T], rstd[:, 0:T], ALU.mult)
                        dve.tensor_tensor(cin[:, t, T + 6:T + 35:4], B[t][:, T:N], rstd[:, T:N], ALU.mult)
                        dve.tensor_tensor(tail[:, ti + t, 0:11], B[t][:, T - 3:N], rstd[:, T - 3:N], ALU.mult)
                        m = dve.tensor_copy(cin[:, t, T + 3:T + 35].rearrange("p (b j) -> p b j", j=4)[:, :, 0:3],
                                            bk[t][:, N:N + 24].rearrange("p (b j) -> p b j", j=3))
                    free(m)
                    dve.wait_ge(pair_free[par], it * (len(ph.pairs) // 2) + (n // 2 + 1))
                    conv(0, 4, lambda j_, t: first_tile + (64 * j_ + t), conv_done)
                elif q.kind == "sc":
                    dve.wait_ge(rows_left, q.arg(it) + 1)
                    for t in range(2):
                        m = dve.tensor_tensor(scb[:, t, :], B[t], rstd[:, :], ALU.mult)
                    free(m)
                    dve.wait_ge(pair_free[par], it * (len(ph.pairs) // 2) + (n // 2 + 1))
                    for t in range(2):
                        m = dve.tensor_tensor(scb[:, t, :], scb[:, t, :], rstd[:, :], ALU.mult)
                    mine.inc(m)
                    mine.settle(dve)
                elif q.kind == "sh":
                    gx = q.arg
                    dve.wait_ge(sct_turned, gx(it) + 1)
                    dve.wait_ge(silu_done, gx(it) * 4 + 4)
                    for t in range(2):
                        dve.tensor_tensor(cin[:, t, 3:3 + T], B[t][:, 0:T], scb[:, t, 0:T], ALU.mult)
                        dve.tensor_tensor(cin[:, t, T + 6:T + 35:4], B[t][:, T:N], scb[:, t, T:N], ALU.mult)
                        dve.tensor_tensor(tail[:, 8 + t, 0:10], B[t][:, T - 2:N], scb[:, t, T - 2:N], ALU.mult)
                        m = dve.tensor_copy(cin[:, t, T + 3:T + 35].rearrange("p (b j) -> p b j", j=4)[:, :, 1:3],
                                            bk[t][:, N:N + 16].rearrange("p (b j) -> p b j", j=2))
                    free(m)
                    dve.wait_ge(pair_free[par], it * (len(ph.pairs) // 2) + (n // 2 + 1))
                    conv(1, 3, lambda j_, t: gx(it) * 2 + (256 + 16 * j_ + t), sconv_done)
                elif q.kind == "sb":
                    i = q.arg(it)
                    dve.wait_ge(yb_ready, i + 1)
                    for t in range(2):
                        m = dve.tensor_tensor(B[t], B[t], rstd[:, :], ALU.mult)
                    mine.inc(m)
                    mine.settle(dve)
                    for t in range(2):
                        m = dve.tensor_tensor(yb[:, 2 * i + t, :], yb[:, 2 * i + t, :], B[t], ALU.mult)
                    free(m)
                elif q.kind in ("gate", "fg", "pg"):
                    for t in range(2):
                        m = dve.tensor_tensor(B[t], B[t], rstd[:, :], ALU.mult)
                    m.then_inc({"gate": gate_scaled, "fg": fg_scaled, "pg": pg_scaled}[q.kind], 1)
                    if q.kind == "fg":
                        freed(dve, ph, it, qi)
                        for t in range(2):
                            m = dve.tensor_tensor(et[:, t, :], et[:, t, :], rstd[:, :], ALU.mult)
                        mine.inc(m)
                        mine.settle(dve)
                    elif q.kind == "pg":
                        dve.wait_ge(pg_done, q.arg(it) + 1)
                        i = q.arg(it)
                        for t in range(2):
                            row = pp[:, ds(i * 2 + t, 1), :].rearrange("p a b -> p (a b)")
                            m = dve.tensor_tensor(et[:, t, :], et[:, t, :], row, ALU.mult)
                        mine.inc(m)
                        mine.settle(dve)
                        for t in range(2):
                            row = h[:, ds(i * 2 + t, 1), :].rearrange("p a b -> p (a b)")
                            m = dve.tensor_tensor(row, row, et[:, t, :], ALU.add)
                        free(m)
                elif q.kind == "yb":
                    for t in range(2):
                        row = sgB[:, ds(q.arg(it) * 2 + t, 1), :].rearrange("p a b -> p (a b)")
                        m = dve.tensor_tensor(row, row, B[t], ALU.mult)
                    free(m)
                elif q.kind == "ya":
                    for t in range(2):
                        row = sgA[:, ds(q.arg(it) * 2 + t, 1), :].rearrange("p a b -> p (a b)")
                        m = dve.tensor_tensor(B[t], B[t], row, ALU.mult)
                    mine.inc(m)
                    mine.settle(dve)
                    for t in range(2):
                        row = sgB[:, ds(q.arg(it) * 2 + t, 1), :].rearrange("p a b -> p (a b)")
                        m = dve.tensor_tensor(row, row, B[t], ALU.add)
                    free(m)
                elif q.kind == "addh":
                    if ph.name == "wo":
                        dve.wait_ge(h_in, 16)
                    for t in range(2):
                        row = h[:, ds(q.arg(it) * 2 + t, 1), :].rearrange("p a b -> p (a b)")
                        m = dve.tensor_tensor(row, row, B[t], ALU.add)
                    free(m)
                elif q.kind == "fu":
                    ax, half, r = q.arg
                    for t in range(2):
                        m = dve.tensor_tensor(et[:, 2 + t, :], B[t], et[:, t, :], ALU.mult)
                    free(m)
                    dve.wait_ge(a_hi, ax(it) + (half * FP + r + 1))
                    freed(dve, ph, it, qi)
                    for t in range(2):
                        m = dve.tensor_tensor(alo[:, ds((ax(it) + r) * 2 + t, 1), :], et[:, 2 + t, :].unsqueeze(1),
                                              f32(ahi[:, ds((ax(it) + r) * 2 + t, 1), :]), ALU.subtract)
                    m.then_inc(a_ready, 1)

            def extra(ph, it, j):
                gr = group_of(ph, it)
                if gr is not None:
                    for step in DVE_STEP.get(j, ()):
                        gdn(step, gr)
                elif ph.name == "first" and j == 9:
                    dve.wait_ge(tok_turned, 1)
                    tv = lambda n: bank[7][:, n * 64:(n + 1) * 64].rearrange("p (c h) -> p c h", c=2)
                    dve.tensor_copy(tok[:, 0, :, :], tv(0))
                    dve.tensor_copy(tok[:, 1, :, :], tv(1))
                    dve.tensor_scalar(tok[:, 2, :, :], tv(1), -1.0, None, ALU.mult)
                    dve.tensor_scalar(tok[:, 3, :, :], tv(2), -1.0, None, ALU.mult)
                    dve.tensor_copy(tok[:, 4, :, :], tv(3))
                    dve.tensor_copy(bc[:, 0:16, :].rearrange("p a b -> p (a b)"), bank[5][:, :])
                    mine.inc(dve.tensor_copy(bc[:, 16, :], bank[6][:, 0:32]))
                    mine.settle(dve)
                elif ph.name in NORM and j == 3:
                    norm_mean(NORM[ph.name])
                elif ph.name == "sb" and j == 1:
                    dve.wait_ge(kq_sum, 1)
                    f = sq2[:, 1, :, :].rearrange("p a b -> p (a b)")
                    mine.inc(dve.tensor_scalar(f, bank[5][:, 0:256], EPS, None, ALU.add))
                    mine.settle(dve)
                    dve.reciprocal(f, f).then_inc(kq_rec, 1)
                elif ph.name == "sb" and j == 3:
                    dve.wait_ge(kq_root, 1)
                    dve.scalar_tensor_tensor(out=kqs[:, :, :, 1], in0=smp[:, 0:HK, :], scalar=QSCALE, in1=sq2[:, 1, 0:HK, :],
                                             op0=ALU.mult, op1=ALU.mult)
                    dve.tensor_tensor(kqs[:, :, :, 0], smp[:, HK:2 * HK, :], sq2[:, 1, HK:2 * HK, :], ALU.mult).then_inc(kq_ready, 1)
                    dve.wait_ge(kq_ready, 1)
                    dve.tensor_tensor(sq2[:, 0, 0:HK, :], kqs[:, :, :, 0], kqs[:, :, :, 1], ALU.mult).then_inc(kq_prod, 1)
                elif ph.name == "yb0" and j == 1:
                    dve.wait_ge(s_used, 2 * NB)
                    R = bank[4][:, :].rearrange("p (b h r) -> p b h r", b=NB, h=HV)
                    step = lambda m: (mine.inc(m), mine.settle(dve))
                    dve.tensor_tensor(so[:, 1, :, :], R[:, :, :, 1], bc[:, 1:1 + NB, :], ALU.mult)
                    step(dve.tensor_tensor(so[:, 0, :, :], R[:, :, :, 0], bc[:, 1:1 + NB, :], ALU.mult))
                    step(dve.tensor_tensor(so[:, 0, :, :], smp[:, 2 * HK:4 * HK, :].rearrange("p h b -> p b h"), so[:, 0, :, :], ALU.subtract))
                    step(dve.tensor_tensor(so[:, 0, :, :], so[:, 0, :, :], bc[:, 1 + NB:1 + 2 * NB, :], ALU.mult))
                    dot = bank[6][:, 0:HK * NB].rearrange("p (k b) -> p b k", b=NB)
                    for r in range(2):
                        m = dve.tensor_tensor(so[:, 2, :, r::2], dot, so[:, 0, :, r::2], ALU.mult)
                    step(m)
                    dve.tensor_tensor(so[:, 2, :, :], so[:, 2, :, :], so[:, 1, :, :], ALU.add).then_inc(d_ready, 1)
                elif ph.name == "yb0" and j == 4:
                    dve.wait_ge(so_sum, 1)
                    f = so[:, 4, :, :].rearrange("p a b -> p (a b)")
                    mine.inc(dve.tensor_scalar(f, bank[7][:, 0:256], 1.0 / P, EPS, ALU.mult, ALU.add))
                    mine.settle(dve)
                    dve.reciprocal(f, f).then_inc(so_rec, 1)
                elif ph.name == "yb0" and j == 6:
                    dve.wait_ge(so_root, 1)
                    mine.inc(dve.scalar_tensor_tensor(out=so[:, 2, :, :], in0=so[:, 2, :, :], scalar=vec[:, 368:369], in1=so[:, 4, :, :],
                                                      op0=ALU.mult, op1=ALU.mult))
                    mine.settle(dve)
                    o = o_all[:, :, T:N]
                    dve.tensor_tensor(o, o, so[:, 2, :, :].rearrange("p b h -> p h b"), ALU.mult).then_inc(so_done, 1)
                elif ph.name in ("ffn0s", "ffn1s") and j % 8 in (3, 4, 5, 6):
                    s, c, quarter = j // 8, int(ph.name[3]), j % 8 - 3
                    dve.wait_ge(n_scaled, it * 8 + (32 * c + 4 * s + quarter + 1))
                    for i in range(4 * quarter, 4 * quarter + 4):
                        m = dve.scalar_tensor_tensor(out=sS[:, s, i, :], in0=sD[:, s, i, :],
                                                     scalar=kqs[:, 8 * c + i // 2, ds(it * 2 + s, 1), 0], in1=sS[:, s, i, :],
                                                     op0=ALU.mult, op1=ALU.add)
                    if quarter == 3:
                        m.then_inc(n_done, 1)

            def work(when, ph, it):
                if when == "body":
                    j = 0
                    for qi, q in enumerate(ph.pairs):
                        for _ in q.kts:
                            split_ahead(ph, it, j)
                            extra(ph, it, j)
                            j += 1
                        evac(q, ph, it, qi, j)
                    return
                name = ph.name
                if name == "first":
                    dve.wait_ge(vec_turned, 1)
                    dve.tensor_copy(vec[:, 0:P], bank[0][:, 0:P])
                    dve.tensor_copy(vec[:, P:2 * P], bank[1][:, 0:P])
                    dve.tensor_copy(vec[:, 2 * P:369], bank[2][:, 0:113]).then_inc(vec_ready, 1)
                    dve.wait_ge(vec_ready, 1)
                    norm_split(0, 304, True)
                    for p in range(AHEAD):
                        split(p, p + 1)
                    dve.wait_ge(consts_ready, 1)
                elif name in ("yb0", "ya0", "ya1", "wo"):
                    src = {"yb0": lambda kt: yb[:, kt, :], "ya0": lambda kt: o_all[:, kt, :],
                           "ya1": lambda kt: o_all[:, DT + kt, :], "wo": lambda kt: sgB[:, kt, :]}[name]
                    if name == "yb0":
                        freed_all(dve, by["gates"])
                    plain_split(XR[{"yb0": "yb", "ya0": "o0", "ya1": "o1", "wo": "mix"}[name]], src)
                elif name == "ffn0r":
                    norm_split(XR["ffn"], 320)
                elif name == "pproj":
                    plain_split(XR["ple_p"], lambda k: bank[5 + k][:, 0:N], PD // P, (phi, plo))
                elif name == "pgate_first":
                    norm_split(XR["ple"], 336)

            walk(dve, work, (mine,), dve_per)
            norm_mean(3)
            for kt in range(DT):
                dve.scalar_tensor_tensor(out=h[:, kt, :], in0=h[:, kt, :], scalar=vec[:, 352 + kt:353 + kt], in1=rstd[:, :],
                                         op0=ALU.mult, op1=ALU.mult).then_inc(y_ready, 1)


_INS = ["x_prompt", "x_sample", "state_gdn", "state_qkv_conv", "state_short_conv", "p_prompt", "p_sample",
        "attn_norm", "w_in", "qkv_conv_w", "a_log", "dt_bias", "gdn_norm", "w_gdn_out", "sconv_w", "w_sconv_out",
        "w_o", "ffn_norm", "w_ffn_gate", "w_ffn_up", "w_ffn_down", "ple_norm", "w_ple_gate", "w_ple_proj", "final_norm"]


def kernel(**inputs):
    import numpy as np
    import concourse.bacc as bacc
    from concourse.bass_utils import run_bass_kernel_spmd

    nc = bacc.Bacc("TRN2", target_bir_lowering=False, num_devices=1)
    arrays, I = {}, {}
    for name in _INS:
        a = np.ascontiguousarray(inputs[name])
        arrays[f"in_{name}"] = a
        I[name] = nc.dram_tensor(f"in_{name}", a.shape, mybir.dt.from_np(a.dtype), kind="ExternalInput").ap()
    one, T, D = inputs["x_prompt"].shape
    depth, NB, HV, DK, DV = inputs["state_gdn"].shape
    QKV, J = inputs["state_qkv_conv"].shape[3], inputs["state_qkv_conv"].shape[2]
    JS = inputs["state_short_conv"].shape[2]
    shapes = {"y_prompt": (one, T, D), "y_sample": (NB, 1, D), "gdn_p": (depth, one, HV, DK, DV), "qkv_p": (depth, one, J, QKV),
              "sc_p": (depth, one, JS, D), "gdn_s": (depth, NB, HV, DK, DV), "qkv_s": (depth, NB, J, QKV), "sc_s": (depth, NB, JS, D)}
    O = {n: nc.dram_tensor(f"out_{n}", s, F32, kind="ExternalOutput").ap() for n, s in shapes.items()}
    trunk(nc, I, O)
    r = run_bass_kernel_spmd(nc, [arrays], core_ids=[0])
    return tuple(r.results[0][f"out_{n}"] for n in shapes)
```
